# Optimizing a Trainium2 kernel written in Bass

```python
import jax, jax.numpy as jnp
from jax import lax
import numpy as np

D_MODEL = 1024
BATCH = 1
SEQ = 256
DEPTH = 1

CHUNK = 64

N_HEADS_A = 16
HEAD_A = D_MODEL // N_HEADS_A
WIDTH_A = N_HEADS_A * HEAD_A
D_DECAY_LORA = 64
D_AAA_LORA = 64
D_GATE_LORA = 160
GN_EPS = 64e-5
SPLITS_A = (WIDTH_A, WIDTH_A, WIDTH_A, D_DECAY_LORA, D_AAA_LORA, D_GATE_LORA)
COLS_A = sum(SPLITS_A)

GMLP_CHUNK = 2 * CHUNK
N_GROUPS_B = 8
GROUP_B = 128
WIDTH_B = N_GROUPS_B * GROUP_B
LN_EPS = 1e-5

N_BRANCHES = 2
IN_COLS = COLS_A + 2 * WIDTH_B + N_BRANCHES * D_MODEL

N_EXPERTS = 32
TOP_K = 4
D_FF_EXPERT = D_MODEL
SWIGLU_LIMIT = 7.0
SWIGLU_ALPHA = 1.702
MOE_BLOCK = 128

RMS_EPS = 1e-5

kernel_name = "hybrid_rwkv7_gmlp_gated_moe_block"

def rms_norm(x, g):
    xf = x.astype(jnp.float32)
    y = xf * lax.rsqrt(jnp.mean(xf * xf, axis=-1, keepdims=True) + RMS_EPS)
    return (y * g.astype(jnp.float32)).astype(x.dtype)

def token_shift(z):
    return jnp.pad(z[:, :-1], ((0, 0), (1, 0), (0, 0)))

def rwkv7_time_mix(z, time_mix, w_decay_up, w0, a_up, a0, g_up, k_k, k_a, r_k, gn_w, gn_b):
    B, S, _ = z.shape
    f32 = jnp.float32
    H, N = N_HEADS_A, HEAD_A
    z = z + (token_shift(z) - z) * time_mix
    idx = [int(i) for i in np.cumsum(SPLITS_A)[:-1]]
    r, k, v, zw, za, zg = jnp.split(z, idx, axis=-1)
    w_log = -jax.nn.softplus(-(w0 + jnp.tanh(zw) @ w_decay_up).astype(f32)) - 0.5
    decay = jnp.exp(-jnp.exp(w_log))
    a = jax.nn.sigmoid((a0 + za @ a_up).astype(f32))
    g = jax.nn.sigmoid(zg) @ g_up

    def heads(t):
        return t.astype(f32).reshape(B, S, H, N)

    r, k, v, decay, a = heads(r), heads(k), heads(v), heads(decay), heads(a)
    kk = k * k_k.astype(f32).reshape(H, N)
    kk = kk / jnp.maximum(jnp.sqrt(jnp.sum(kk * kk, axis=-1, keepdims=True)), 1e-12)
    k = k * (1.0 + (a - 1.0) * k_a.astype(f32).reshape(H, N))

    def step(state, inp):
        r_t, k_t, v_t, w_t, kk_t, a_t = inp
        sa = jnp.einsum('bhij,bhj->bhi', state, -kk_t)
        state = (state * w_t[:, :, None, :]
                 + sa[..., None] * (kk_t * a_t)[:, :, None, :]
                 + v_t[..., None] * k_t[:, :, None, :])
        y_t = jnp.einsum('bhij,bhj->bhi', state, r_t)
        return state, y_t

    xs = tuple(jnp.moveaxis(t, 1, 0) for t in (r, k, v, decay, kk, a))
    _, y = lax.scan(step, jnp.zeros((B, H, N, N), f32), xs)
    y = jnp.moveaxis(y, 0, 1)
    mean = jnp.mean(y, axis=-1, keepdims=True)
    var = jnp.mean(jnp.square(y - mean), axis=-1, keepdims=True)
    y = ((y - mean) * lax.rsqrt(var + GN_EPS) * gn_w.astype(f32).reshape(H, N)
         + gn_b.astype(f32).reshape(H, N))
    y = y + jnp.sum(r * k * r_k.astype(f32).reshape(H, N), axis=-1, keepdims=True) * v
    y = y.reshape(B, S, WIDTH_A) * g.astype(f32)
    return y.astype(z.dtype)

def gmlp_spatial_gate(u_raw, v_raw, ln_v_g, ln_v_b, w_spatial, b_spatial):
    B, S, _ = u_raw.shape
    f32 = jnp.float32
    u = jax.nn.gelu(u_raw.astype(f32), approximate=False)
    vf = jax.nn.gelu(v_raw.astype(f32), approximate=False)
    mean = jnp.mean(vf, axis=-1, keepdims=True)
    var = jnp.mean(jnp.square(vf - mean), axis=-1, keepdims=True)
    vn = (vf - mean) * lax.rsqrt(var + LN_EPS) * ln_v_g.astype(f32) + ln_v_b.astype(f32)
    vc = vn.reshape(B, S // GMLP_CHUNK, GMLP_CHUNK, N_GROUPS_B, GROUP_B)
    mask = jnp.tril(jnp.ones((GMLP_CHUNK, GMLP_CHUNK), dtype=bool))
    ws = jnp.where(mask[None], w_spatial.astype(f32), 0.0)
    s = jnp.einsum('gij,bcjgd->bcigd', ws, vc) + b_spatial.astype(f32).T[:, :, None]
    return (u * s.reshape(B, S, WIDTH_B)).astype(u_raw.dtype)

def moe_ffn(h, w_router, b_router, w_gate_up, b_gate_up, w_down, b_down):
    B, S, D = h.shape
    T = B * S
    n_assign = T * TOP_K
    n_blocks = n_assign // MOE_BLOCK + N_EXPERTS
    xt = h.reshape(T, D)
    logits = (xt @ w_router + b_router).astype(jnp.float32)
    top_v, top_i = lax.top_k(logits, TOP_K)
    gates = jax.nn.softmax(top_v, axis=-1)
    flat_e = top_i.reshape(-1).astype(jnp.int32)
    flat_tok = jnp.arange(n_assign, dtype=jnp.int32) // TOP_K
    order = jnp.argsort(flat_e, stable=True)
    sorted_e = flat_e[order]
    counts = jnp.bincount(flat_e, length=N_EXPERTS).astype(jnp.int32)
    padded = (counts + MOE_BLOCK - 1) // MOE_BLOCK * MOE_BLOCK
    pad_end = jnp.cumsum(padded)
    pad_start = pad_end - padded
    grp_start = jnp.cumsum(counts) - counts
    dest = pad_start[sorted_e] + jnp.arange(n_assign, dtype=jnp.int32) - grp_start[sorted_e]
    slot_tok = jnp.zeros((n_blocks * MOE_BLOCK,), jnp.int32).at[dest].set(flat_tok[order])
    block_start = jnp.arange(n_blocks, dtype=jnp.int32) * MOE_BLOCK
    block_expert = jnp.minimum(jnp.searchsorted(pad_end, block_start, side='right'),
                               N_EXPERTS - 1).astype(jnp.int32)

    def expert_block(args):
        tok, e = args
        hgu = xt[tok] @ w_gate_up[e] + b_gate_up[e]
        gate = jnp.minimum(hgu[:, 0::2], SWIGLU_LIMIT)
        up = jnp.clip(hgu[:, 1::2], -SWIGLU_LIMIT, SWIGLU_LIMIT)
        act = gate * jax.nn.sigmoid(SWIGLU_ALPHA * gate) * (up + 1.0)
        return act @ w_down[e] + b_down[e]

    y_slots = lax.map(expert_block, (slot_tok.reshape(n_blocks, MOE_BLOCK), block_expert))
    y_slots = y_slots.reshape(n_blocks * MOE_BLOCK, D)
    slot_of_assign = jnp.zeros((n_assign,), jnp.int32).at[order].set(dest)
    y_sel = y_slots[slot_of_assign].reshape(T, TOP_K, D)
    out = jnp.einsum('tk,tkd->td', gates.astype(h.dtype), y_sel)
    return out.reshape(B, S, D)

def setup_inputs(seed: int = 0) -> dict:
    key = jax.random.key(seed)
    ks = jax.random.split(key, 32)
    L, D = DEPTH, D_MODEL
    f32 = jnp.float32

    def nrm(k, shape, scale):
        return jax.random.normal(k, shape, f32) * scale

    return {
        "x": jax.random.normal(ks[0], (BATCH, SEQ, D), f32),
        "norm1_g": 1.0 + nrm(ks[1], (L, D), 0.05),
        "w_in": nrm(ks[2], (L, D, IN_COLS), D ** -0.5),
        "b_gate": nrm(ks[3], (L, N_BRANCHES * D), 0.1),
        "time_mix": jax.random.uniform(ks[4], (L, COLS_A), f32),
        "w_decay_up": nrm(ks[5], (L, D_DECAY_LORA, WIDTH_A), D_DECAY_LORA ** -0.5),
        "w0": jax.random.uniform(ks[6], (L, WIDTH_A), f32, minval=-5.0, maxval=-1.0),
        "a_up": nrm(ks[7], (L, D_AAA_LORA, WIDTH_A), D_AAA_LORA ** -0.5),
        "a0": nrm(ks[8], (L, WIDTH_A), 0.1),
        "g_up": nrm(ks[9], (L, D_GATE_LORA, WIDTH_A), D_GATE_LORA ** -0.5),
        "k_k": 0.85 + nrm(ks[10], (L, WIDTH_A), 0.05),
        "k_a": 1.0 + nrm(ks[11], (L, WIDTH_A), 0.05),
        "r_k": nrm(ks[12], (L, WIDTH_A), 0.1),
        "gn_w": 1.0 + nrm(ks[13], (L, WIDTH_A), 0.05),
        "gn_b": nrm(ks[14], (L, WIDTH_A), 0.02),
        "ln_v_g": 1.0 + nrm(ks[15], (L, WIDTH_B), 0.05),
        "ln_v_b": nrm(ks[16], (L, WIDTH_B), 0.02),
        "w_spatial": nrm(ks[17], (L, N_GROUPS_B, GMLP_CHUNK, GMLP_CHUNK), GMLP_CHUNK ** -0.5),
        "b_spatial": 1.0 + nrm(ks[18], (L, N_GROUPS_B, GMLP_CHUNK), 0.1),
        "w_out": nrm(ks[19], (L, D, D), D ** -0.5),
        "norm2_g": 1.0 + nrm(ks[20], (L, D), 0.05),
        "w_router": nrm(ks[21], (L, D, N_EXPERTS), D ** -0.5),
        "b_router": nrm(ks[22], (L, N_EXPERTS), 0.01),
        "w_gate_up": nrm(ks[23], (L, N_EXPERTS, D, 2 * D_FF_EXPERT), D ** -0.5),
        "b_gate_up": nrm(ks[24], (L, N_EXPERTS, 2 * D_FF_EXPERT), 0.02),
        "w_down": nrm(ks[25], (L, N_EXPERTS, D_FF_EXPERT, D), D_FF_EXPERT ** -0.5),
        "b_down": nrm(ks[26], (L, N_EXPERTS, D), 0.02),
        "norm_f_g": 1.0 + nrm(ks[27], (D,), 0.05),
    }

def reference(x, norm1_g, w_in, b_gate, time_mix, w_decay_up, w0, a_up, a0, g_up, k_k, k_a, r_k,
              gn_w, gn_b, ln_v_g, ln_v_b, w_spatial, b_spatial, w_out, norm2_g, w_router, b_router,
              w_gate_up, b_gate_up, w_down, b_down, norm_f_g):
    for l in range(DEPTH):
        h = rms_norm(x, norm1_g[l])
        z = h @ w_in[l]
        z_a, u_raw, v_raw, gate_logits = jnp.split(
            z, [COLS_A, COLS_A + WIDTH_B, COLS_A + 2 * WIDTH_B], axis=-1)
        y_a = rwkv7_time_mix(z_a, time_mix[l], w_decay_up[l], w0[l], a_up[l], a0[l], g_up[l],
                             k_k[l], k_a[l], r_k[l], gn_w[l], gn_b[l])
        y_b = gmlp_spatial_gate(u_raw, v_raw, ln_v_g[l], ln_v_b[l], w_spatial[l], b_spatial[l])
        gates = jax.nn.sigmoid(gate_logits + b_gate[l])
        g_a, g_b = jnp.split(gates, N_BRANCHES, axis=-1)
        x = x + (g_a * y_a + g_b * y_b) @ w_out[l]
        x = x + moe_ffn(rms_norm(x, norm2_g[l]), w_router[l], b_router[l], w_gate_up[l],
                        b_gate_up[l], w_down[l], b_down[l])
    return rms_norm(x, norm_f_g)


_drawn_inputs = setup_inputs


def setup_inputs(seed=0):
    import zlib

    import numpy as np

    out = dict(_drawn_inputs(seed))
    spreads = {}
    factors = {'a0': 2.706, 'gn_b': 3.046, 'ln_v_b': 4.28, 'b_gate_up': 5.598, 'b_down': 6.461}
    for name, (base, spread) in spreads.items():
        noise = np.random.default_rng([zlib.crc32(name.encode()), seed]).standard_normal(out[name].shape)
        drawn = base * np.exp(spread * noise) if base else spread * noise
        out[name] = __import__('jax').numpy.asarray(drawn.astype(out[name].dtype))
    for name, factor in factors.items():
        out[name] = (out[name] * factor).astype(out[name].dtype)
    return out
```

```python
import numpy as np
import concourse.bass as bass
from concourse import mybir
from contextlib import ExitStack

T, D = 256, 1024
P = 128
KT = D // P
TB = T // P
HEADS, HD = 16, 64
CH = 64
NCH = T // CH
PAIRS = HEADS * NCH
LORA = 64
GLORA = 160
COLS_A = 3 * D + 2 * LORA + GLORA
GROUPS = 8
EXPERTS, TOPK = 32, 4
FF = D
SLOTS = 64
KAPPA = float(np.exp(-0.5))
RMS_EPS, LN_EPS, GN_EPS = 1e-5, 1e-5, 64e-5
LIMIT, ALPHA = 7.0, 1.702

VEC, VROWS = {}, 0
for _name, _n in (("norm1", KT), ("mix_r", KT), ("mix_k", KT), ("mix_v", KT), ("mix_lora", 3),
                  ("w0", KT), ("a0", KT), ("k_k", KT), ("k_a", KT), ("r_k", KT), ("b_sp", GROUPS)):
    VEC[_name] = (VROWS, _n)
    VROWS += _n

CST, _at = {}, 0
for _name, _n in (("ident", P), ("gmask", P), ("headones", P), ("before", P), ("ones", P), ("causal", P),
                  ("carry", T), ("iota_slot", 2 * SLOTS), ("merge", SLOTS), ("iota_exp", EXPERTS), ("of_head", 2)):
    CST[_name] = (_at, _n)
    _at += _n
CST_W = _at


def constants():
    c = np.zeros((P, CST_W), np.float32)
    p = np.arange(P)[:, None]
    j = np.arange(P)[None, :]

    def put(name, a):
        at, n = CST[name]
        c[:, at:at + n] = a
    put("ident", p == j)
    s, t = p % CH, j % CH
    put("gmask", np.where(j < CH, s < t, s <= t))
    put("headones", p // HD == j // HD)
    put("before", p < j)
    put("ones", 1.0)
    put("causal", p <= j)
    put("carry", (np.arange(T)[None, :] % CH) != 0)
    put("iota_slot", (np.arange(2 * SLOTS) % SLOTS)[None, :])
    put("merge", (p - SLOTS == np.arange(SLOTS)[None, :]) | (p < 2))
    put("iota_exp", np.arange(EXPERTS)[None, :])
    put("of_head", p // HD == np.arange(2)[None, :])
    return c


def build(nc, cst, x, norm1_g, w_in, b_gate, time_mix, w_decay_up, w0, a_up, a0, g_up, k_k, k_a, r_k,
          gn_w, gn_b, ln_v_g, ln_v_b, w_spatial, b_spatial, w_out, norm2_g, w_router, b_router,
          w_gate_up, b_gate_up, w_down, b_down, norm_f_g, out, dbg=None):
    fp32, f32r, i32, u32 = mybir.dt.float32, mybir.dt.float32r, mybir.dt.int32, mybir.dt.uint32
    ALU, ACT, AX = mybir.AluOpType, mybir.ActivationFunctionType, mybir.AxisListType
    V, S, G, E = nc.vector, nc.scalar, nc.gpsimd, nc.tensor
    MUL, ADD, SUB = ALU.mult, ALU.add, ALU.subtract

    ctx = ExitStack()
    with ctx:
        KB = 1024
        BASE = 16512
        TOP = 229344

        def at(name, off, cols, dt=fp32, parts=P):
            assert BASE + off + 4 * cols <= TOP, (name, off, cols)
            return nc.alloc_sbuf_tensor_at(name, [parts, cols], dt, offset=BASE + off)

        class Map:
            def __init__(self, lo, hi):
                self.at, self.hi = lo, hi

            def take(self, name, cols, dt=fp32, parts=P):
                t = at(name, self.at, cols, dt, parts)
                self.at += -(-4 * cols // 32) * 32
                assert self.at <= self.hi, (name, self.at, self.hi)
                return t

        END = TOP - BASE
        keep = Map(0, END)
        cs_ = keep.take("consts", CST_W)
        vec = keep.take("vec", VROWS)
        xacc = keep.take("xacc", TB * D)
        small = keep.take("small", 512)
        WBUF = keep.at
        wa = at("wa", WBUF, 8 * KT * P)
        wb = at("wb", WBUF, 2 * KT * 512)
        bc = at("bc", WBUF + 32 * KB, 4 * D)
        RING, PIECE = 6, 2 * FF
        ring = at("ring", WBUF, RING * PIECE)
        FRONT = WBUF + 48 * KB

        m = Map(FRONT, END)
        hT = m.take("hT", KT * T)
        arg = m.take("arg", PAIRS * P)
        gup = m.take("gup", PAIRS * P, parts=CH)
        bk = m.take("bk", PAIRS * HD)
        vtok = m.take("vtok", TB * D)
        sg = m.take("sg", 2 * T)
        bonus = m.take("bonus", TB * HEADS)
        plast = m.take("plast", PAIRS, parts=CH)
        m1 = Map(m.at, END)
        upw = m1.take("upw", D)
        zp = [[m1.take(f"zp{i}{b}", T + 2) for i in range(3)] for b in range(2)]
        zs = [[m1.take(f"zs{i}{b}", T) for i in range(3)] for b in range(2)]
        qb = [m1.take(f"q{b}", T) for b in range(2)]
        ar = [m1.take(f"ar{b}", 2 * T) for b in range(2)]
        bf = [m1.take(f"bf{b}", 2 * T) for b in range(2)]
        dec, decp, inv, nrm, sqb, tmp, csum, csump, kr, kp = (
            m1.take(n, T) for n in "dec decp inv nrm sqb tmp csum csump kr kp".split())
        sw = at("sw", WBUF + 32 * KB, KT * T)
        sa = at("sa", WBUF + 40 * KB, KT * T)
        xn = at("xn", FRONT + 8 * KB, TB * D)
        xj = at("xj", FRONT + 24 * KB, D)
        vrow = at("vrow", FRONT + 32 * KB, P)
        m2 = Map(m.at, END)
        vsb = m2.take("vsb", TB * D)
        mb = m2.take("mb", TB * D)
        LATE = m2.at
        al = m2.take("al", 1024)
        xl = m2.take("xl", 1024)
        prod = m2.take("prod", 1024)
        x1w = m2.take("x1w", PAIRS * 32, parts=CH)
        wsr = m2.take("wsr", GROUPS * P)
        wst = m2.take("wst", GROUPS * P)
        m3 = Map(LATE, END)
        zst = m3.take("zst", NCH * HEADS * HD)
        uv = m3.take("uv", HEADS * HD)
        rhs = m3.take("rhs", HEADS * HD, parts=CH)
        ysb = at("ysb", FRONT, TB * D)
        m4 = Map(FRONT + 8 * KB, FRONT + 88 * KB)
        gu1 = m4.take("gu1", D)
        gu2 = m4.take("gu2", D, parts=32)
        yt = m4.take("yt", D)
        mT = m4.take("mT", KT * T)
        wr = m4.take("wr", KT * EXPERTS)
        br = m4.take("br", EXPERTS, parts=1)
        h2 = m4.take("h2", TB * D)
        lg, el, mask = (m4.take(n, TB * EXPERTS) for n in ("lg", "el", "mask"))
        mx = m4.take("mx", TB * 8)
        ix = m4.take("ix", TB * 8, u32)
        ixf = m4.take("ixf", TB * 8)
        bd = m4.take("bd", D, parts=EXPERTS)
        gt = m4.take("gt", T, parts=EXPERTS)
        bg = m4.take("bg", 2 * FF, parts=EXPERTS)
        bgh = m4.take("bgh", 2 * FF, f32r, parts=EXPERTS)
        bgl = m4.take("bgl", 2 * FF, f32r, parts=EXPERTS)
        NB = 4
        SPLIT = 118 * KB
        m5 = Map(FRONT + SPLIT, END)
        h2h = m5.take("h2h", TB * D, f32r)
        h2l = m5.take("h2l", TB * D, f32r)
        posm = m5.take("posm", TB * EXPERTS)
        gate = m5.take("gate", TB * EXPERTS)
        npass = m5.take("npass", 8, i32)
        gs = m5.take("gs", 8)
        nf = m5.take("nf", D)
        m5 = Map(FRONT, FRONT + SPLIT)
        wh = [m5.take(f"wh{b}", PIECE, f32r) for b in range(NB)]
        wl = [m5.take(f"wl{b}", PIECE, f32r) for b in range(NB)]
        S2 = 2 * SLOTS
        oh = m5.take("oh", TB * S2, f32r)
        oht = m5.take("oht", 4 * T, f32r)
        xe = m5.take("xe", D, parts=SLOTS)
        xs = [m5.take(f"xs{b}", KT * S2, f32r) for b in range(2)]
        xf = [m5.take(f"xf{b}", SLOTS) for b in range(2)]
        gc = m5.take("gc", FF, parts=SLOTS)
        uc = m5.take("uc", FF, parts=SLOTS)
        sgm = m5.take("sgm", FF, parts=SLOTS)
        acts = gc
        as_ = m5.take("as", KT * S2, f32r)
        af = m5.take("af", 2 * SLOTS)
        yh = m5.take("yh", D, f32r)
        yl = m5.take("yl", D, f32r)
        comb = m5.take("comb", 2 * FF, f32r)
        mrg = m5.take("mrg", SLOTS, f32r)
        zero = nc.alloc_sbuf_tensor_at("zero", [1, 512], mybir.dt.bfloat16, offset=BASE + m5.at)
        m5.at += KB

        def C(name, rows=slice(0, P)):
            a, n = CST[name]
            return cs_[rows, a:a + n]

        def vcol(name, i=0):
            return vec[:, VEC[name][0] + i:VEC[name][0] + i + 1]

        scr_a = nc.dram_tensor("scr_a", [P, 32, 32], fp32).ap()
        scr_x = nc.dram_tensor("scr_x", [P, 32, 32], fp32).ap()
        scr_b = nc.dram_tensor("scr_b", [EXPERTS, 2, 2 * FF], f32r).ap()

        ps = ctx.enter_context(nc.psum_tensor("ps", [P, 8 * 512], fp32))

        def bank(b, lo=0, n=512, parts=slice(0, P)):
            return ps[parts, 512 * b + lo:512 * b + lo + n]

        def sem(name):
            return ctx.enter_context(nc.semaphore(name))

        stage_end = [sem(f"stage_end{i + 1}") for i in range(5)]
        misc = [sem(f"misc_loaded{i}") for i in range(2)]
        x_in = sem("x_in")
        wa_full = [sem(f"wa_full{i}") for i in range(8)]
        wb_full = [sem(f"wb_full{i}") for i in range(2)]
        dve_chain, act_chain = sem("dve_chain"), sem("act_chain")
        names = ("act_ready arg_top at_done at_hi at_lo b_hi b_split b_st bc_in bd_done comb_used cb_ready csum_ready dec_ready "
                 "e_out eps_ready feat_ready fin_ready ga_done gate_pre gate_ready gate_sig gc_ready "
                 "glora_done gn_sqrt gram_done gram_out gt_ps gt_ready gu_read mrg_ready  h2_hi h2_ps h2_ready "
                 "h_ps h_ready hi_ready lanes_done lanes_ld lanes_st late_in lg_done ln_mean ln_sq ln_sqrt lo_act "
                 "lo_mixed mT_ready m_ps m_ready mask_ready neg_max nf_in norm_done nrm_ready o_out oh_ready "
                 "ones_ready pads pb_done pb_out split_used pos_done pos_moved proj_done q_ready r_done r_out s_done "
                 "s_out sc_added sc_done sig_done sp_done sp_out sq_ready stored sumsq tr_done tr_out u_done u_out "
                 "ug_ready up_done up_sig uv_v v_put vec_ps vec_ready vn_ready w1_done w1_out ws_in wst_copied wst_ps "
                 "wst_ready x1_ready x21_done x21_out x_st zeroed xe_ready xn_ready xrms xt_done xt_hi "
                 "xt_in xt_lo y_done y_hi y_lo y_out yc_ready yc_sq yvar z_copied zk_ready zr_ready zs_used").split()
        sm = {n: sem(n) for n in names}
        bias_in = sem("bias_in")
        ring_full = [sem(f"ring_full{i}") for i in range(RING)]
        ring_read = [sem(f"ring_read{i}") for i in range(RING)]

        class Chain:
            def __init__(self, eng, s):
                self.eng, self.s, self.n = eng, s, 0

            def __call__(self, ins):
                self.n += 1
                ins.then_inc(self.s, 1)
                self.eng.wait_ge(self.s, self.n)

        class Own:
            def __init__(self, eng):
                self.eng, self.n = eng, {}

            def __call__(self, name):
                self.n[name] = self.n.get(name, 0) + 1
                self.eng.wait_ge(sm[name], self.n[name])

        def meet(eng, k):
            eng.drain().then_inc(stage_end[k - 1], 1)
            eng.wait_ge(stage_end[k - 1], 4 if k < 4 else 5)

        block = ctx.enter_context(nc.Block())

        a_cols = [(3 * D, P), (3 * D + P, P), (3 * D + 2 * P, 32)]
        for c in range(KT):
            a_cols += [(D + c * P, P), (c * P, P), (2 * D + c * P, P)]
        NA = len(a_cols)
        b_cols = [COLS_A + D, COLS_A + D + 512, COLS_A, COLS_A + 512,
                  COLS_A + 3 * D, COLS_A + 3 * D + 512, COLS_A + 2 * D, COLS_A + 2 * D + 512]
        NBC = len(b_cols)

        UNSPLIT = (3, 9)
        GU_UNSPLIT, DOWN_UNSPLIT = UNSPLIT
        PER_PASS = EXPERTS * 12
        SPLITS = 12 - len(UNSPLIT)
        GU_SPLITS = KT - 1

        def passes(eng):
            return eng.value_load(npass[0:1, 0:1], min_val=1, max_val=T // SLOTS)

        def eno(p, e):
            return p * EXPERTS + e

        def ring_at(p, e, s):
            edge = isinstance(e, int)
            o = s if edge and e == 0 else s - 12 if edge and e == EXPERTS else s - 4
            return o % RING, p * (PER_PASS // RING) + 2 * e + (o // RING + 1)

        def split_no(p, e, s):
            before = sum(1 for i in range(s) if i not in UNSPLIT)
            edge = isinstance(e, int)
            o = before if edge and e == 0 else before - SPLITS if edge and e == EXPERTS else before + GU_SPLITS - SPLITS
            return p * (EXPERTS * SPLITS) + SPLITS * e + o

        def split_buf(e, s, u):
            return split_no(0, e if isinstance(e, int) else 4 + u, s) % NB

        def last_gu(p, e):
            return split_no(p, e, KT - 1) + 1

        def last_down(p, e):
            return split_no(p, e + 1, 11) + 1

        def col(t, tb, e):
            return t[:, bass.ds(tb * EXPERTS + e, 1)] if not isinstance(e, int) else t[:, tb * EXPERTS + e:tb * EXPERTS + e + 1]

        SPLITTER = {0: ["oh"], 1: ["y"], 3: ["sc0"], 4: ["sc1"], 5: ["at"], 6: ["ga"], 8: ["xt"], 10: ["low"], 11: ["glu", "act"]}
        MULTIPLIER = {1: ["sc0"], 2: ["sc1"], 3: ["at"], 4: ["ga"], 6: ["xt"], 8: ["low"]}
        RUNS = {"oh": (-1, 30), "ga": (-1, 30), "xt": (-1, 30), "y": (2, 33), "sc0": (2, 33), "sc1": (2, 33),
                "at": (1, 32), "low": (0, 31), "glu": (0, 31), "act": (0, 31)}

        def iteration(p, e, u, like, step, task, plan):
            for s in range(12):
                if (0 <= like <= 31) if s < KT else (1 <= like <= 32):
                    step(p, e, s, u)
                for what in plan.get(s, ()):
                    if RUNS[what][0] <= like <= RUNS[what][1]:
                        task(p, e, what, u)

        def moe_steps(eng, step, task, tensor=False):
            plan = MULTIPLIER if tensor else SPLITTER
            with eng.Fori(0, passes(eng)) as p:
                for e in (-1, 0, 1):
                    iteration(p, e, e % 4, e, step, task, plan)
                with eng.Fori(0, 7) as i:
                    for v in range(4):
                        iteration(p, i * 4 + (2 + v), (2 + v) % 4, 5, step, task, plan)
                for e in range(30, 34):
                    iteration(p, e, e % 4, e, step, task, plan)
                if not tensor:
                    task(p, EXPERTS + 1, "next", 0)

        @block.sync
        def _(sp):
            w_in_v = w_in[0].rearrange("(k p) n -> p k n", p=P)
            wa_v = wa[:, :].rearrange("p (s k n) -> p s k n", s=8, k=KT)
            wb_v = wb[:, :].rearrange("p (s k n) -> p s k n", s=2, k=KT)
            sp.dma_start(xacc[:, 0:D], x[0, 0:P, :]).then_inc(x_in, 16)
            sp.dma_start(xacc[:, D:2 * D], x[0, P:T, :]).then_inc(x_in, 16)
            sp.dma_start(cs_[:, :], cst).then_inc(misc[0], 16)
            for n, (c0, w) in enumerate(a_cols):
                if n >= 8:
                    sp.wait_ge(sm["proj_done"], n - 7)
                sp.dma_start(wa_v[:, n % 8, :, 0:w], w_in_v[:, :, c0:c0 + w]).then_inc(wa_full[n % 8], 16)
            sp.wait_ge(sm["proj_done"], NA)
            w_out_v = w_out[0].rearrange("(k p) n -> p k n", p=P)
            for n in range(NBC + 2):
                if n >= 2:
                    sp.wait_ge(sm["pb_done"], 2 * (n - 1))
                src = w_in_v[:, :, b_cols[n]:b_cols[n] + 512] if n < NBC else w_out_v[:, :, 512 * (n - NBC):512 * (n - NBC + 1)]
                sp.dma_start(wb_v[:, n % 2, :, :], src).then_inc(wb_full[n % 2], 16)
            meet(sp, 4)
            gu_v = w_gate_up[0].rearrange("e (k p) n -> e k p n", p=P)
            dn_v = w_down[0].rearrange("e (j two p) n -> e j p two n", p=P, two=2)

            def fetch(p, e, s, src):
                slot, fill = ring_at(p, e, s)
                sp.wait_ge(ring_read[slot], fill)
                sp.dma_start(ring[:, slot * PIECE:(slot + 1) * PIECE].rearrange("p (a n) -> p a n", a=src.shape[1]), src).then_inc(ring_full[slot], 16)

            def weights(p, e, gu=True, down=True):
                if gu:
                    for k in range(KT):
                        fetch(p, e, k, gu_v[bass.ds(e, 1), k, :, :].rearrange("e p n -> p e n"))
                if down:
                    for j in range(4):
                        fetch(p, e, KT + j, dn_v[bass.ds(e - 1, 1), j, :, :, :].rearrange("e p two n -> p (e two) n"))

            with sp.Fori(0, passes(sp)) as p:
                weights(p, 0, down=False)
                with sp.Fori(1, EXPERTS) as e:
                    weights(p, e)
                weights(p, EXPERTS, gu=False)
            meet(sp, 5)
            sp.wait_ge(sm["fin_ready"], 2)
            for tb in range(TB):
                sp.dma_start(out[0, tb * P:(tb + 1) * P, :], xacc[:, tb * D:(tb + 1) * D]).then_inc(sm["stored"], 16)
            sp.wait_ge(sm["stored"], 32)

        @block.gpsimd
        def _(pool):
            nc.gpsimd.memset(vrow[0:VROWS, :], 0.0).then_inc(sm["zeroed"], 1)
            pool.wait_ge(sm["zeroed"], 1)

            def rows(name, src, n):
                r = VEC[name][0]
                pool.dma_start(vrow[r:r + n, :], src.rearrange("(r p) -> r p", p=P)).then_inc(misc[1], 16)
            rows("norm1", norm1_g[0], KT)
            rows("mix_r", time_mix[0, 0:D], KT)
            rows("mix_k", time_mix[0, D:2 * D], KT)
            rows("mix_v", time_mix[0, 2 * D:3 * D], KT)
            rows("mix_lora", time_mix[0, 3 * D:3 * D + 2 * P], 2)
            r = VEC["mix_lora"][0] + 2
            pool.dma_start(vrow[r:r + 1, 0:32], time_mix[0:1, 3 * D + 2 * P:COLS_A]).then_inc(misc[1], 16)
            for name, src in (("w0", w0), ("a0", a0), ("k_k", k_k), ("k_a", k_a), ("r_k", r_k)):
                rows(name, src[0], KT)
            r = VEC["b_sp"][0]
            pool.dma_start(vrow[r:r + GROUPS, :], b_spatial[0]).then_inc(misc[1], 16)
            pool.dma_start(upw[0:LORA, :], w_decay_up[0]).then_inc(misc[1], 16)
            pool.dma_start(upw[LORA:P, :], a_up[0]).then_inc(misc[1], 16)
            meet(pool, 1)
            gup_v = gup[:, :].rearrange("s (q t) -> s q t", q=PAIRS)
            for half in range(2):
                h = slice(32 * half, 32 * half + 32)
                pool.dma_start(scr_a[half * PAIRS:(half + 1) * PAIRS].rearrange("l s t -> s l t"),
                               gup_v[h, :, h]).then_inc(sm["lanes_st"], 16)
            pool.wait_ge(sm["lanes_st"], 32)
            pool.dma_start(al[:, :], scr_a.rearrange("l s t -> l (s t)")).then_inc(sm["lanes_ld"], 16)
            pool.dma_start(wsr[:, :].rearrange("i (g j) -> i g j", g=GROUPS),
                           w_spatial[0].rearrange("g i j -> i g j")).then_inc(sm["ws_in"], 16)
            for i, src in enumerate((ln_v_g[0], ln_v_b[0], b_gate[0, 0:D], b_gate[0, D:2 * D])):
                pool.dma_start(bc[:, i * D:(i + 1) * D], src.partition_broadcast(P)).then_inc(sm["bc_in"], 16)
            pool.wait_ge(sm["lanes_done"], 1)
            pool.dma_start(scr_x.rearrange("l s t -> l (s t)"), xl[:, :]).then_inc(sm["x_st"], 16)
            pool.wait_ge(sm["x_st"], 16)
            for half in range(2):
                h = slice(32 * half, 32 * half + 32)
                pool.dma_start(gup_v[h, :, h], scr_x[half * PAIRS:(half + 1) * PAIRS].rearrange("l s t -> s l t")).then_inc(sm["xt_in"], 16)
            meet(pool, 2)
            for i, src in enumerate((gn_w[0], gn_b[0], norm2_g[0])):
                pool.dma_start(bc[:, i * D:(i + 1) * D], src.partition_broadcast(P)).then_inc(sm["bc_in"], 16)
            meet(pool, 3)
            pool.dma_start(gu1[:, :], g_up[0, 0:P, :]).then_inc(sm["late_in"], 16)
            pool.dma_start(gu2[:, :], g_up[0, P:GLORA, :]).then_inc(sm["late_in"], 16)
            pool.dma_start(wr[:, :].rearrange("p (k n) -> p k n", k=KT),
                           w_router[0].rearrange("(k p) n -> p k n", p=P)).then_inc(sm["late_in"], 16)
            pool.dma_start(br[:, :], b_router).then_inc(sm["late_in"], 16)
            pool.dma_start(bd[:, :], b_down[0]).then_inc(sm["late_in"], 16)
            pool.dma_start(bg[:, :], b_gate_up[0]).then_inc(sm["late_in"], 16)
            pool.wait_ge(sm["b_split"], 1)
            pool.dma_start(scr_b[:, 0, :], bgh[:, :]).then_inc(sm["b_st"], 16)
            pool.dma_start(scr_b[:, 1, :], bgl[:, :]).then_inc(sm["b_st"], 16)
            pool.wait_ge(sm["b_st"], 32)
            meet(pool, 4)
            nc.gpsimd.memset(zero[:, :], 0.0).then_inc(sm["zeroed"], 1)
            nc.gpsimd.memset(comb[0:SLOTS, :].bitcast(fp32), 0.0).then_inc(sm["zeroed"], 1)
            pool.dma_start(nf[:, :], norm_f_g.partition_broadcast(P)).then_inc(sm["nf_in"], 16)
            pool.wait_ge(sm["zeroed"], 3)

            def bias(p, e):
                pool.wait_ge(sm["comb_used"], eno(p, e) + 1)
                pool.dma_start(comb[0:2, :], scr_b[bass.ds(e, 1), :, :].rearrange("e two n -> (e two) n")).then_inc(bias_in, 16)

            with pool.Fori(0, passes(pool)) as p:
                with pool.Fori(0, EXPERTS) as e:
                    bias(p, e)
            meet(pool, 5)

        @block.scalar
        def _(act):
            act_ = S.activation
            link, own = Chain(act, act_chain), Own(act)
            act.wait_ge(x_in, 32)
            for tb in range(TB):
                if tb:
                    act.wait_ge(sm["sumsq"], tb)
                act_(xj[:, :], xacc[:, tb * D:(tb + 1) * D], ACT.Square, accum_out=small[:, tb:tb + 1]).then_inc(sm["sumsq"], 1)
                own("sumsq")
            act.wait_ge(sm["sumsq"], 2)
            act.wait_ge(misc[0], 16)
            act.wait_ge(sm["eps_ready"], 1)
            act_(small[:, 2:4], small[:, 0:2], ACT.Sqrt, scale=1.0 / D, bias=small[:, 60:61]).then_inc(sm["xrms"], 1)
            own("xrms")
            n_z = [0]

            def zcopy(dst, rows=P):
                n = n_z[0]
                act.wait_ge(sm["proj_done"], n + 1)
                act_(dst[0:rows, 1:T + 1], bank(n % 2, 0, T, slice(0, rows)), ACT.Copy).then_inc(sm["z_copied"], 1)
                own("z_copied")
                n_z[0] += 1

            act.wait_ge(sm["pads"], 1)
            for i in range(3):
                zcopy(zp[0][i], 32 if i == 2 else P)
            act.wait_ge(sm["lo_mixed"], 1)
            act_(zs[0][0][0:LORA, :], zs[0][0][0:LORA, :], ACT.Tanh).then_inc(sm["lo_act"], 1)
            own("lo_act")
            act.wait_ge(sm["lo_mixed"], 3)
            link(act_(sg[:, 0:T], zs[0][1][:, :], ACT.Sigmoid))
            act_(sg[0:32, T:2 * T], zs[0][2][0:32, :], ACT.Sigmoid).then_inc(sm["lo_act"], 1)
            own("lo_act")
            for c in range(KT):
                act.wait_ge(sm["up_done"], c + 1)
                cols = slice(c * T, (c + 1) * T)
                link(act_(sw[:, cols], bank(2 + 2 * (c % 2), 0, T), ACT.Sigmoid, bias=vcol("w0", c)))
                act_(sa[:, cols], bank(3 + 2 * (c % 2), 0, T), ACT.Sigmoid, bias=vcol("a0", c)).then_inc(sm["up_sig"], 1)
                own("up_sig")

            def tile_copies(c):
                b = c % 2
                act.wait_ge(sm["feat_ready"], c + 1)
                for hh in range(2):
                    rows = slice(HD * hh, HD * hh + HD)
                    q0 = (2 * c + hh) * NCH
                    link(act_(arg[0:HD, q0 * P:(q0 + NCH) * P], ar[b][rows, :], ACT.Copy))
                    act_(plast[0:HD, q0:q0 + NCH], dec[rows, CH - 1:T:CH], ACT.Copy).then_inc(sm["arg_top"], 1)
                    own("arg_top")
                act.wait_ge(sm["tr_done"], c + 1)
                for hh in range(2):
                    q0 = (2 * c + hh) * NCH
                    link(act_(bk[:, q0 * HD:(q0 + NCH) * HD].rearrange("p (q j) -> p q j", q=NCH),
                         bank(6).rearrange("p (q h j) -> p q h j", q=NCH, h=2)[:, :, hh, :], ACT.Copy))
                act_(vtok[:, :].rearrange("p (b n) -> p b n", b=TB)[:, :, c * P:(c + 1) * P],
                     bank(7, 0, 2 * P).rearrange("p (b n) -> p b n", b=TB), ACT.Copy).then_inc(sm["tr_out"], 1)
                own("tr_out")

            for c in range(KT):
                b = c % 2
                if c >= 2:
                    act.wait_ge(sm["zs_used"], c - 1)
                for i in (1, 0, 2):
                    zcopy(zp[b][i])
                act.wait_ge(sm["zk_ready"], c + 1)
                act_(sqb[:, :], zs[b][1][:, :], ACT.Square, scale=vcol("k_k", c)).then_inc(sm["sq_ready"], 1)
                own("sq_ready")
                act.wait_ge(sm["norm_done"], c + 1)
                act_(nrm[:, :], bank(2, 0, T), ACT.Sqrt).then_inc(sm["nrm_ready"], 1)
                own("nrm_ready")
                if c:
                    tile_copies(c - 1)
                act.wait_ge(sm["csum_ready"], c + 1)
                link(act_(dec[:, :], csum[:, :], ACT.Exp, scale=-KAPPA))
                link(act_(decp[:, :], csump[:, :], ACT.Exp, scale=-KAPPA))
                act_(inv[:, :], csum[:, :], ACT.Exp, scale=KAPPA).then_inc(sm["dec_ready"], 1)
                own("dec_ready")
            tile_copies(KT - 1)
            link(act_(bonus[:, :], bank(3, 0, TB * HEADS), ACT.Copy))
            meet(act, 1)
            act.wait_ge(sm["wst_ps"], 1)
            act_(wst[:, :], ps[:, 4 * 512:6 * 512], ACT.Copy).then_inc(sm["wst_copied"], 1)
            own("wst_copied")
            for n in range(4):
                for tb in range(TB):
                    m_ = 2 * n + tb
                    act.wait_ge(sm["pb_done"], m_ + 1)
                    dst = (vsb if n < 2 else mb)[:, tb * D + 512 * (n % 2):tb * D + 512 * (n % 2) + 512]
                    act_(dst, bank(m_ % 4), ACT.Gelu).then_inc(sm["pb_out"], 1)
                    own("pb_out")
            for tb in range(TB):
                act.wait_ge(sm["ln_mean"], tb + 1)
                act_(al[:, :], vsb[:, tb * D:(tb + 1) * D], ACT.Square, accum_out=small[:, 10 + tb:11 + tb]).then_inc(sm["ln_sq"], 1)
                own("ln_sq")
                act.wait_ge(sm["ln_sq"], tb + 1)
            act_(small[:, 12:14], small[:, 10:12], ACT.Sqrt, scale=1.0 / D, bias=small[:, 61:62]).then_inc(sm["ln_sqrt"], 1)
            own("ln_sqrt")
            for n in range(4, 8):
                for tb in range(TB):
                    m_ = 2 * (n - 4) + tb
                    act.wait_ge(sm["gate_pre"], m_ + 1)
                    if n < 6:
                        gb = prod[:, (m_ % 2) * 512:(m_ % 2) * 512 + 512]
                        act_(gb, gb, ACT.Sigmoid).then_inc(sm["gate_sig"], 1)
                        own("gate_sig")
                    else:
                        ga = vsb[:, tb * D + 512 * (n % 2):tb * D + 512 * (n % 2) + 512]
                        act_(ga, ga, ACT.Sigmoid).then_inc(sm["gate_sig"], 1)
                        own("gate_sig")
            for r in range(4):
                act.wait_ge(sm["w1_done"], r + 1)
                act_(x1w[32:64, r * 512:(r + 1) * 512], bank(4, 0, 512, slice(32, 64)), ACT.Copy).then_inc(sm["w1_out"], 1)
                own("w1_out")
            meet(act, 2)
            vt_odd = vtok[:, :].rearrange("p (b n) -> p b n", b=TB)
            for c in range(NCH):
                rows = slice(CH * (c % 2), CH * (c % 2) + CH)
                act_(zst[CH:P, c * D:(c + 1) * D], vt_odd[rows, c // 2, :], ACT.Copy).then_inc(sm["v_put"], 1)
                own("v_put")
            for c in range(NCH):
                if c:
                    act.wait_ge(sm["y_done"], 2 * c)
                act.wait_ge(sm["v_put"], NCH)
                act_(uv[CH:P, :], zst[CH:P, c * D:(c + 1) * D], ACT.Copy).then_inc(sm["uv_v"], 1)
                own("uv_v")
                for g in range(2):
                    act.wait_ge(sm["r_done"], 2 * c + g + 1)
                    act_(rhs[:, g * 512:(g + 1) * 512], bank(g, 0, 512, slice(0, CH)), ACT.Copy).then_inc(sm["r_out"], 1)
                    own("r_out")
                if c % 2:
                    act.wait_ge(sm["y_done"], 2 * c + 2)
                    act_(ysb[:, (c // 2) * D:(c // 2 + 1) * D], ps[:, 6 * 512:8 * 512], ACT.Copy).then_inc(sm["y_out"], 1)
                    own("y_out")
            meet(act, 3)
            for tb in range(TB):
                act.wait_ge(sm["yc_ready"], tb + 1)
                act_(yt[:, :], ysb[:, tb * D:(tb + 1) * D], ACT.Square).then_inc(sm["yc_sq"], 1)
                own("yc_sq")
                act.wait_ge(sm["yvar"], tb + 1)
                act_(small[:, 80 + 16 * tb:96 + 16 * tb], small[:, 112 + 16 * tb:128 + 16 * tb], ACT.Sqrt, scale=1.0 / HD, bias=small[:, 62:63]).then_inc(sm["gn_sqrt"], 1)
                own("gn_sqrt")
            act.wait_ge(sm["late_in"], 96)
            act_(bgh[:, :], bg[:, :], ACT.Copy).then_inc(sm["b_hi"], 1)
            own("b_hi")
            for tb in range(TB):
                act.wait_ge(sm["m_ps"], tb + 1)
                act_(mT[:, :].rearrange("p (k t) -> p k t", k=KT)[:, :, tb * P:(tb + 1) * P],
                     ps[:, 4 * 512:6 * 512].rearrange("p (k t) -> p k t", k=KT), ACT.Copy).then_inc(sm["mT_ready"], 1)
                own("mT_ready")
            for tb in range(TB):
                act.wait_ge(sm["o_out"], 4)
                act_(yt[:, :], xacc[:, tb * D:(tb + 1) * D], ACT.Square, accum_out=small[:, 20 + tb:21 + tb]).then_inc(sm["sumsq"], 1)
                own("sumsq")
            act_(small[:, 22:24], small[:, 20:22], ACT.Sqrt, scale=1.0 / D, bias=small[:, 60:61]).then_inc(sm["xrms"], 1)
            own("xrms")
            for tb in range(TB):
                act.wait_ge(sm["h2_ps"], tb + 1)
                act_(mT[:, :].rearrange("p (k t) -> p k t", k=KT)[:, :, tb * P:(tb + 1) * P],
                     ps[:, 4 * 512:6 * 512].rearrange("p (k t) -> p k t", k=KT), ACT.Copy).then_inc(sm["mT_ready"], 1)
                own("mT_ready")
            for tb in range(TB):
                act_(h2h[:, tb * D:(tb + 1) * D], h2[:, tb * D:(tb + 1) * D], ACT.Copy).then_inc(sm["h2_hi"], 1)
                own("h2_hi")
            for tb in range(TB):
                act.wait_ge(sm["neg_max"], tb + 1)
                e_ = slice(tb * EXPERTS, (tb + 1) * EXPERTS)
                act_(el[:, e_], lg[:, e_], ACT.Exp, bias=small[:, 30 + tb:31 + tb]).then_inc(sm["e_out"], 1)
                own("e_out")
            meet(act, 4)

            act_(mrg[:, :], C("merge"), ACT.Copy).then_inc(sm["mrg_ready"], 1)
            halves = lambda t: t[:, :].rearrange("p (k two s) -> p k two s", k=KT, two=2)
            tiles = lambda a: a.rearrange("p (k s) -> p k s", k=KT)

            def hi(p, e, s, u):
                if s in UNSPLIT:
                    return
                slot, fill = ring_at(p, e, s)
                buf = split_buf(e, s, u)
                act.wait_ge(ring_full[slot], fill * 16)
                act.wait_ge(sm["split_used"], split_no(p, e, s) + 1)
                act_(wh[buf][:, :], ring[:, slot * PIECE:(slot + 1) * PIECE], ACT.Copy).then_inc(sm["hi_ready"], 1)

            def task(p, e, what, u):
                if what == "y":
                    act.wait_ge(sm["split_used"], last_down(p, e - 2) + NB)
                    act_(yh[:, :], ps[:, 4 * 512:6 * 512], ACT.Copy, scale=gs[:, (u - 2) % 4:(u - 2) % 4 + 1]).then_inc(sm["y_hi"], 1)
                if what == "at":
                    act.wait_ge(sm["at_done"], eno(p, e))
                    f0 = 2 * (DOWN_UNSPLIT - KT)
                    act_(af[:, :], bank(6, f0 * SLOTS, 2 * SLOTS), ACT.Copy)
                    act_(halves(as_)[:, :, 0, :], tiles(bank(6)), ACT.Copy).then_inc(sm["at_hi"], 1)
                if what == "ga":
                    act.wait_ge(sm["ga_done"], eno(p, e) + 2)
                    act_(xe[:, :], ps[0:SLOTS, 6 * 512:8 * 512], ACT.Copy).then_inc(sm["xe_ready"], 1)
                if what == "xt":
                    act.wait_ge(sm["xt_done"], eno(p, e) + 2)
                    b, q = (u + 1) % 2, (u + 1) % 4
                    act_(oht[:, q * T:(q + 1) * T], bank(7, 0, T), ACT.Copy)
                    act_(gs[:, q:q + 1], bank(7, T, 1), ACT.Copy)
                    act_(xf[b][:, :], bank(6, GU_UNSPLIT * SLOTS, SLOTS), ACT.Copy)
                    act_(halves(xs[b])[:, :, 0, :], tiles(bank(6)), ACT.Copy).then_inc(sm["xt_hi"], 1)
                if what == "low":
                    act.wait_ge(sm["split_used"], last_gu(p, e) + NB)
                    act_(comb[SLOTS:P, :], ps[SLOTS:P, 0:4 * 512], ACT.Copy).then_inc(sm["cb_ready"], 1)
                if what == "glu":
                    act.wait_ge(sm["gc_ready"], eno(p, e) + 1)
                    act_(sgm[:, :], gc[:, :], ACT.Sigmoid, scale=ALPHA).then_inc(sm["sig_done"], 1)

            moe_steps(act, hi, task)
            meet(act, 5)
            for tb in range(TB):
                act_(ring[:, 0:D], xacc[:, tb * D:(tb + 1) * D], ACT.Square, accum_out=small[:, 20 + tb:21 + tb]).then_inc(sm["sumsq"], 1)
                own("sumsq")
            act_(small[:, 22:24], small[:, 20:22], ACT.Sqrt, scale=1.0 / D, bias=small[:, 60:61]).then_inc(sm["xrms"], 1)

        @block.vector
        def _(dve):
            link, own = Chain(dve, dve_chain), Own(dve)
            link(V.memset(small[:, 60:61], RMS_EPS))
            link(V.memset(small[:, 61:62], LN_EPS))
            V.memset(small[:, 62:63], GN_EPS).then_inc(sm["eps_ready"], 1)
            own("eps_ready")
            for b in range(2):
                for i in range(3):
                    last = V.memset(zp[b][i][:, 0:1], 0.0)
            last.then_inc(sm["pads"], 1)
            own("pads")
            dve.wait_ge(sm["xrms"], 1)
            link(V.reciprocal(small[:, 4:6], small[:, 2:4]))
            for tb in range(TB):
                V.tensor_scalar(xn[:, tb * D:(tb + 1) * D], xacc[:, tb * D:(tb + 1) * D], small[:, 4 + tb:5 + tb], None, MUL).then_inc(sm["xn_ready"], 1)
                own("xn_ready")
            dve.wait_ge(sm["vec_ps"], 1)
            V.tensor_copy(vec[:, :], bank(4, 0, VROWS)).then_inc(sm["vec_ready"], 1)
            own("vec_ready")
            dve.wait_ge(sm["vec_ready"], 1)
            for tb in range(TB):
                dve.wait_ge(sm["h_ps"], tb + 1)
                V.tensor_tensor(hT[:, :].rearrange("p (k t) -> p k t", k=KT)[:, :, tb * P:(tb + 1) * P],
                                ps[:, tb * 1024:(tb + 1) * 1024].rearrange("p (k t) -> p k t", k=KT),
                                vec[:, 0:KT].unsqueeze(2).to_broadcast([P, KT, P]), MUL).then_inc(sm["h_ready"], 1)
                own("h_ready")

            def mix(src, dst, col, count, rows=P, done=None):
                dve.wait_ge(sm["z_copied"], count)
                r = slice(0, rows)
                link(V.tensor_tensor(tmp[r, :], src[r, 0:T], src[r, 1:T + 1], SUB))
                ins = V.scalar_tensor_tensor(dst[r, :], tmp[r, :], col[r, :], src[r, 1:T + 1], MUL, ADD)
                ins.then_inc(sm[done], 1)
                own(done)

            for i in range(3):
                mix(zp[0][i], zs[0][i], vcol("mix_lora", i), i + 1, 32 if i == 2 else P, "lo_mixed")
            dve.wait_ge(sm["up_sig"], KT)

            def gram_evac(c):
                dve.wait_ge(sm["gram_done"], c + 1)
                for hh in range(2):
                    q0 = (2 * c + hh) * NCH
                    for rows, dst in ((slice(0, CH), gup), (slice(CH, P), arg)):
                        last = V.tensor_tensor(dst[rows, q0 * P:(q0 + NCH) * P].rearrange("p (q t) -> p q t", q=NCH),
                                               bank(4 + hh, 0, 512, rows).rearrange("p (q t) -> p q t", q=NCH),
                                               C("gmask", rows).unsqueeze(1).to_broadcast([CH, NCH, P]), MUL)
                last.then_inc(sm["gram_out"], 1)
                own("gram_out")

            for c in range(KT):
                b = c % 2
                zk, zr, zv = zs[b][1], zs[b][0], zs[b][2]
                cols = slice(c * T, (c + 1) * T)
                if c >= 2:
                    dve.wait_ge(sm["tr_done"], c - 1)
                mix(zp[b][1], zk, vcol("mix_k", c), 3 + 3 * c + 1, P, "zk_ready")
                mix(zp[b][0], zr, vcol("mix_r", c), 3 + 3 * c + 2, P, "zr_ready")
                link(V.tensor_tensor_scan(csum[:, :], C("carry"), sw[:, cols], 0.0, MUL, ADD))
                link(V.tensor_tensor(csump[:, :], csum[:, :], sw[:, cols], SUB))
                dve.sem_inc(sm["csum_ready"], 1)
                dve.wait_ge(sm["zk_ready"], c + 1)
                dve.wait_ge(sm["zr_ready"], c + 1)
                link(V.tensor_scalar(tmp[:, :], sa[:, cols], 1.0, vcol("k_a", c), SUB, MUL))
                link(V.scalar_tensor_tensor(kp[:, :], tmp[:, :], 1.0, zk[:, :], ADD, MUL))
                V.scalar_tensor_tensor(qb[b][:, :], zr[:, :], vcol("r_k", c), kp[:, :], MUL, MUL).then_inc(sm["q_ready"], 1)
                own("q_ready")
                mix(zp[b][2], zv, vcol("mix_v", c), 3 + 3 * c + 3, P, "zs_used")
                dve.wait_ge(sm["nrm_ready"], c + 1)
                link(V.tensor_scalar(nrm[:, :], nrm[:, :], 1e-12, None, ALU.max))
                link(V.reciprocal(nrm[:, :], nrm[:, :]))
                link(V.scalar_tensor_tensor(kr[:, :], zk[:, :], vcol("k_k", c), nrm[:, :], MUL, MUL))
                link(V.tensor_tensor(tmp[:, :], kr[:, :], sa[:, cols], MUL))
                dve.wait_ge(sm["dec_ready"], c + 1)
                ar_v = ar[b][:, :].rearrange("p (q w t) -> p q w t", q=NCH, w=2)
                bf_v = bf[b][:, :].rearrange("p (q w t) -> p q w t", q=NCH, w=2)
                q3 = lambda a: a.rearrange("p (q t) -> p q t", q=NCH)
                link(V.scalar_tensor_tensor(ar_v[:, :, 0, :], q3(kr[:, :]), -1.0, q3(decp[:, :]), MUL, MUL))
                link(V.tensor_tensor(ar_v[:, :, 1, :], q3(zr[:, :]), q3(dec[:, :]), MUL))
                link(V.tensor_tensor(bf_v[:, :, 0, :], q3(tmp[:, :]), q3(inv[:, :]), MUL))
                V.tensor_tensor(bf_v[:, :, 1, :], q3(kp[:, :]), q3(inv[:, :]), MUL).then_inc(sm["feat_ready"], 1)
                own("feat_ready")
                if c:
                    gram_evac(c - 1)
            gram_evac(KT - 1)
            meet(dve, 1)
            xl_v = xl[:, :].rearrange("p (n s) -> p n s", n=32)
            al_v = al[:, :].rearrange("p (s t) -> p s t", s=32)
            link(V.memset(xl[:, :], 0.0))
            link(V.memset(xl[:, 0:1024:33], 1.0))
            dve.wait_ge(sm["lanes_ld"], 16)
            for t in range(1, 32):
                pr = prod[:, 0:t * t].rearrange("p (n s) -> p n s", n=t)
                link(V.tensor_tensor(pr, xl_v[:, 0:t, 0:t], al_v[:, 0:t, t].unsqueeze(1).to_broadcast([P, t, t]), MUL))
                link(V.tensor_reduce(xl_v[:, 0:t, t], pr, AX.X, ADD))
            dve.sem_inc(sm["lanes_done"], 1)
            dve.wait_ge(sm["wst_copied"], 1)
            V.tensor_tensor(wst[:, :].rearrange("p (g i) -> p g i", g=GROUPS), wst[:, :].rearrange("p (g i) -> p g i", g=GROUPS),
                            C("causal").unsqueeze(1).to_broadcast([P, GROUPS, P]), MUL).then_inc(sm["wst_ready"], 1)
            own("wst_ready")
            dve.wait_ge(sm["bc_in"], 64)
            dve.wait_ge(sm["pb_out"], 4)
            for tb in range(TB):
                v_ = vsb[:, tb * D:(tb + 1) * D]
                link(V.tensor_reduce(small[:, 14 + tb:15 + tb], v_, AX.X, ADD))
                link(V.tensor_scalar(small[:, 16 + tb:17 + tb], small[:, 14 + tb:15 + tb], 1.0 / D, None, MUL))
                V.tensor_scalar(v_, v_, small[:, 16 + tb:17 + tb], None, SUB).then_inc(sm["ln_mean"], 1)
                own("ln_mean")
            dve.wait_ge(sm["ln_sqrt"], 1)
            link(V.reciprocal(small[:, 18:20], small[:, 12:14]))
            for tb in range(TB):
                v_ = vsb[:, tb * D:(tb + 1) * D]
                link(V.scalar_tensor_tensor(v_, v_, small[:, 18 + tb:19 + tb], bc[:, 0:D], MUL, MUL))
                V.tensor_tensor(v_, v_, bc[:, D:2 * D], ADD).then_inc(sm["vn_ready"], 1)
                own("vn_ready")
            dve.wait_ge(sm["pb_out"], 8)
            for tb in range(TB):
                dve.wait_ge(sm["sp_done"], tb + 1)
                for g in range(GROUPS):
                    o = mb[:, tb * D + g * P:tb * D + (g + 1) * P]
                    last = V.scalar_tensor_tensor(o, ps[:, 6 * 512 + g * P:6 * 512 + (g + 1) * P], vcol("b_sp", g), o, ADD, MUL)
                last.then_inc(sm["sp_out"], 1)
                own("sp_out")
            dve.wait_ge(sm["sp_out"], 2)
            for n in range(4, 8):
                for tb in range(TB):
                    m_ = 2 * n + tb
                    dve.wait_ge(sm["pb_done"], m_ + 1)
                    dst = (prod[:, (m_ % 2) * 512:(m_ % 2) * 512 + 512] if n < 6
                           else vsb[:, tb * D + 512 * (n % 2):tb * D + 512 * (n % 2) + 512])
                    bias = bc[:, (3 if n < 6 else 2) * D + 512 * (n % 2):(3 if n < 6 else 2) * D + 512 * (n % 2) + 512]
                    V.tensor_tensor(dst, bank(m_ % 4), bias, ADD).then_inc(sm["gate_pre"], 1)
                    own("gate_pre")
                    if n < 6:
                        dve.wait_ge(sm["gate_sig"], m_ - 8 + 1)
                        o = mb[:, tb * D + 512 * (n % 2):tb * D + 512 * (n % 2) + 512]
                        link(V.tensor_tensor(o, o, dst, MUL))
            dve.wait_ge(sm["xt_in"], 32)
            gup_q = gup[:, :].rearrange("s (q t) -> s q t", q=PAIRS)
            V.transpose(x1w[0:32, :].rearrange("s (q t) -> s q t", q=PAIRS), gup_q[0:32, :, 0:32]).then_inc(sm["x1_ready"], 1)
            own("x1_ready")
            for r in range(4):
                dve.wait_ge(sm["x21_done"], r + 1)
                V.tensor_copy(gup_q[0:32, 16 * r:16 * r + 16, 32:64],
                              bank(5, 0, 512, slice(0, 32)).rearrange("s (q t) -> s q t", q=16)).then_inc(sm["x21_out"], 1)
                own("x21_out")
            meet(dve, 2)
            for g in range(2):
                V.memset(zst[0:HD, g * 512:(g + 1) * 512], 0.0).then_inc(sm["s_out"], 1)
                own("s_out")
            for c in range(NCH):
                for g in range(2):
                    dve.wait_ge(sm["u_done"], 2 * c + g + 1)
                    if c:
                        dve.wait_ge(sm["y_done"], 2 * c)
                    V.tensor_copy(uv[0:CH, g * 512:(g + 1) * 512], bank(2 + g, 0, 512, slice(0, CH))).then_inc(sm["u_out"], 1)
                    own("u_out")
                if c == NCH - 1:
                    break
                for g in range(2):
                    dve.wait_ge(sm["s_done"], 2 * c + g + 1)
                    s_in = zst[0:HD, c * D + g * 512:c * D + (g + 1) * 512]
                    s_out = zst[0:HD, (c + 1) * D + g * 512:(c + 1) * D + (g + 1) * 512]
                    link(V.tensor_tensor(s_out, bank(4 + g, 0, 512, slice(0, HD)), s_in, ADD))
                    pl = plast[:, :].rearrange("j (h c) -> j h c", c=NCH)[:, 8 * g:8 * g + 8, c]
                    so = s_out.rearrange("j (h i) -> j h i", h=8)
                    V.tensor_tensor(so, so, pl.unsqueeze(2).to_broadcast([HD, 8, HD]), MUL).then_inc(sm["s_out"], 1)
                    own("s_out")
            meet(dve, 3)
            h3 = lambda a: a.rearrange("p (h i) -> p h i", h=HEADS)
            per_head = lambda a: a.unsqueeze(2).to_broadcast([P, HEADS, HD])
            dve.wait_ge(sm["bc_in"], 112)
            dve.wait_ge(sm["late_in"], 96)
            for tb in range(TB):
                y = ysb[:, tb * D:(tb + 1) * D]
                mean, var, std = small[:, 144:160], small[:, 112 + 16 * tb:128 + 16 * tb], small[:, 80 + 16 * tb:96 + 16 * tb]
                link(V.tensor_reduce(mean, h3(y), AX.X, ADD))
                link(V.tensor_scalar(mean, mean, 1.0 / HD, None, MUL))
                V.tensor_tensor(h3(y), h3(y), per_head(mean), SUB).then_inc(sm["yc_ready"], 1)
                own("yc_ready")
                dve.wait_ge(sm["yc_sq"], tb + 1)
                V.tensor_reduce(var, h3(yt[:, :]), AX.X, ADD).then_inc(sm["yvar"], 1)
                own("yvar")
                dve.wait_ge(sm["gn_sqrt"], tb + 1)
                link(V.reciprocal(std, std))
                link(V.tensor_tensor(h3(y), h3(y), per_head(std), MUL))
                link(V.tensor_tensor(y, y, bc[:, 0:D], MUL))
                link(V.tensor_tensor(y, y, bc[:, D:2 * D], ADD))
                v_ = vtok[:, tb * D:(tb + 1) * D]
                link(V.tensor_tensor(h3(v_), h3(v_), per_head(bonus[:, tb * HEADS:(tb + 1) * HEADS]), MUL))
                link(V.tensor_tensor(y, y, v_, ADD))
                dve.wait_ge(sm["glora_done"], tb + 1)
                link(V.tensor_tensor(y, y, ps[:, tb * 1024:(tb + 1) * 1024], MUL))
                link(V.tensor_tensor(y, y, vsb[:, tb * D:(tb + 1) * D], MUL))
                V.tensor_tensor(y, y, mb[:, tb * D:(tb + 1) * D], ADD).then_inc(sm["m_ready"], 1)
                own("m_ready")
            dve.wait_ge(sm["b_hi"], 1)
            V.tensor_tensor(bgl[:, :], bg[:, :], bgh[:, :].bitcast(fp32), SUB).then_inc(sm["b_split"], 1)
            own("b_split")
            for i in range(4):
                half, tb = i // 2, i % 2
                dve.wait_ge(sm["pb_done"], 2 * NBC + i + 1)
                o = xacc[:, tb * D + 512 * half:tb * D + 512 * half + 512]
                V.tensor_tensor(o, o, bank(i), ADD).then_inc(sm["o_out"], 1)
                own("o_out")
            dve.wait_ge(sm["xrms"], 2)
            link(V.reciprocal(small[:, 24:26], small[:, 22:24]))
            for tb in range(TB):
                V.scalar_tensor_tensor(h2[:, tb * D:(tb + 1) * D], xacc[:, tb * D:(tb + 1) * D], small[:, 24 + tb:25 + tb],
                                       bc[:, 2 * D:3 * D], MUL, MUL).then_inc(sm["h2_ready"], 1)
                own("h2_ready")
            for tb in range(TB):
                dve.wait_ge(sm["h2_hi"], tb + 1)
                c_ = slice(tb * D, (tb + 1) * D)
                link(V.tensor_tensor(h2l[:, c_], h2[:, c_], h2h[:, c_].bitcast(fp32), SUB))
            for tb in range(TB):
                e_ = slice(tb * EXPERTS, (tb + 1) * EXPERTS)
                m8, i8, f8 = mx[:, 8 * tb:8 * tb + 8], ix[:, 8 * tb:8 * tb + 8], ixf[:, 8 * tb:8 * tb + 8]
                dve.wait_ge(sm["lg_done"], tb + 1)
                link(V.tensor_copy(lg[:, e_], bank(6 * tb, 0, EXPERTS)))
                link(V.max(m8, lg[:, e_]))
                V.tensor_scalar(small[:, 30 + tb:31 + tb], m8[:, 0:1], -1.0, None, MUL).then_inc(sm["neg_max"], 1)
                own("neg_max")
                link(V.max_index(i8, m8, lg[:, e_]))
                link(V.tensor_copy(f8, i8))
                link(V.tensor_scalar(mask[:, e_], C("iota_exp"), f8[:, 0:1], None, ALU.is_equal))
                for k in range(1, TOPK):
                    ins = V.scalar_tensor_tensor(mask[:, e_], C("iota_exp"), f8[:, k:k + 1], mask[:, e_], ALU.is_equal, ADD)
                    link(ins)
                dve.sem_inc(sm["mask_ready"], 1)
                dve.wait_ge(sm["e_out"], tb + 1)
                link(V.tensor_tensor(el[:, e_], el[:, e_], mask[:, e_], MUL))
                link(V.tensor_reduce(small[:, 32 + tb:33 + tb], el[:, e_], AX.X, ADD))
                link(V.reciprocal(small[:, 34 + tb:35 + tb], small[:, 32 + tb:33 + tb]))
                V.tensor_scalar(gate[:, e_], el[:, e_], small[:, 34 + tb:35 + tb], None, MUL).then_inc(sm["gate_ready"], 1)
                own("gate_ready")
            dve.wait_ge(sm["pos_done"], 1)
            link(V.scalar_tensor_tensor(posm[:, :], bank(1, 0, TB * EXPERTS), 1.0, mask[:, :], ADD, MUL))
            link(V.tensor_scalar(posm[:, :], posm[:, :], -1.0, None, ADD))
            link(V.reduce_max(small[:, 40:41], bank(1, 128, EXPERTS), AX.X))
            link(V.tensor_scalar(small[:, 41:42], small[:, 40:41], SLOTS + 0.5, 1.0, ALU.is_gt, ADD))
            for k in range(2, T // SLOTS):
                link(V.scalar_tensor_tensor(small[:, 41:42], small[:, 40:41], k * SLOTS + 0.5, small[:, 41:42], ALU.is_gt, ADD))
            link(V.tensor_copy(npass[:, 0:1], small[:, 41:42]))
            dve.wait_ge(sm["gt_ps"], 1)
            V.tensor_copy(gt[:, :], bank(7, 0, T, slice(0, EXPERTS))).then_inc(sm["gt_ready"], 1)
            own("gt_ready")
            dve.wait_ge(sm["bd_done"], 1)
            V.tensor_tensor(xacc[:, :], xacc[:, :], ps[:, 2 * 512:6 * 512], ADD).then_inc(sm["sc_added"], 1)
            own("sc_added")
            for slot in range(RING):
                dve.sem_inc(ring_read[slot], 1)
            meet(dve, 4)

            halves = lambda t: t[:, :].rearrange("p (k two s) -> p k two s", k=KT, two=2)
            tiles = lambda a: a.rearrange("p (k s) -> p k s", k=KT)

            def lo(p, e, s, u):
                if s in UNSPLIT:
                    return
                slot, fill = ring_at(p, e, s)
                buf = split_buf(e, s, u)
                dve.wait_ge(sm["hi_ready"], split_no(p, e, s) + 1)
                V.tensor_tensor(wl[buf][:, :], ring[:, slot * PIECE:(slot + 1) * PIECE], wh[buf][:, :].bitcast(fp32), SUB).then_inc(ring_read[slot], 1)

            def task(p, e, what, u):
                n = eno(p, e)
                if what == "oh":
                    if not (isinstance(e, int) and e < 0):
                        dve.wait_ge(sm["xt_done"], n + 1)
                    else:
                        dve.wait_ge(sm["pos_moved"], p + 1)
                    for tb in range(TB):
                        last = V.tensor_scalar(oh[:, tb * S2:(tb + 1) * S2], C("iota_slot"),
                                               col(posm, tb, e + 1), None, ALU.is_equal)
                    last.then_inc(sm["oh_ready"], 1)
                if what == "y":
                    dve.wait_ge(sm["y_hi"], n - 1)
                    V.scalar_tensor_tensor(yl[:, :], ps[:, 4 * 512:6 * 512], gs[:, (u - 2) % 4:(u - 2) % 4 + 1],
                                           yh[:, :].bitcast(fp32), MUL, SUB).then_inc(sm["y_lo"], 1)
                if what in ("sc0", "sc1"):
                    tb = int(what[2])
                    dve.wait_ge(sm["sc_done"], 2 * n - 4 + tb + 1)
                    dve.wait_ge(sm["sc_added"], 2 * n - 4 + tb + 1)
                    o = xacc[:, tb * D:(tb + 1) * D]
                    V.tensor_tensor(o, o, ps[:, 6 * 512:8 * 512], ADD).then_inc(sm["sc_added"], 1)
                if what == "at":
                    dve.wait_ge(sm["at_hi"], n)
                    V.tensor_tensor(halves(as_)[:, :, 1, :], tiles(bank(6)), halves(as_)[:, :, 0, :].bitcast(fp32), SUB).then_inc(sm["at_lo"], 1)
                if what == "xt":
                    dve.wait_ge(sm["xt_hi"], n + 2)
                    b = (u + 1) % 2
                    V.tensor_tensor(halves(xs[b])[:, :, 1, :], tiles(bank(6)), halves(xs[b])[:, :, 0, :].bitcast(fp32), SUB).then_inc(sm["xt_lo"], 1)
                if what == "glu":
                    dve.wait_ge(sm["comb_used"], n + 2)
                    pairs = ps[0:SLOTS, 0:4 * 512].rearrange("p (f two) -> p two f", two=2)
                    V.tensor_scalar(gc[:, :], pairs[:, 0, :], LIMIT, None, ALU.min).then_inc(sm["gc_ready"], 1)
                    V.tensor_scalar(uc[:, :], pairs[:, 1, :], LIMIT, -LIMIT, ALU.min, ALU.max).then_inc(sm["gu_read"], 1)
                if what == "act":
                    dve.wait_ge(sm["gu_read"], n + 2)
                    V.scalar_tensor_tensor(uc[:, :], uc[:, :], 1.0, gc[:, :], ADD, MUL).then_inc(sm["ug_ready"], 1)
                    dve.wait_ge(sm["ug_ready"], n + 1)
                    dve.wait_ge(sm["sig_done"], n + 1)
                    V.tensor_tensor(acts[:, :], uc[:, :], sgm[:, :], MUL).then_inc(sm["act_ready"], 1)
                if what == "next":
                    V.tensor_scalar(posm[:, :], posm[:, :], float(-SLOTS), None, ADD).then_inc(sm["pos_moved"], 1)

            dve.sem_inc(sm["pos_moved"], 1)
            dve.sem_inc(sm["gu_read"], 1)
            moe_steps(dve, lo, task)
            meet(dve, 5)
            dve.wait_ge(sm["nf_in"], 16)
            dve.wait_ge(sm["xrms"], 3)
            link(V.reciprocal(small[:, 24:26], small[:, 22:24]))
            for tb in range(TB):
                o = xacc[:, tb * D:(tb + 1) * D]
                V.scalar_tensor_tensor(o, o, small[:, 24 + tb:25 + tb], nf[:, :], MUL, MUL).then_inc(sm["fin_ready"], 1)

        @block.tensor
        def _(pe):
            mm, tr = E.matmul, E.transpose
            ident = C("ident")
            hv = hT[:, :].rearrange("p (k t) -> p k t", k=KT)
            pe.wait_ge(misc[0], 16)
            pe.wait_ge(misc[1], 16 * 14)
            tr(bank(4, 0, VROWS), vrow[0:VROWS, :], ident[0:VROWS, 0:VROWS]).then_inc(sm["vec_ps"], 1)
            for tb in range(TB):
                pe.wait_ge(sm["xn_ready"], tb + 1)
                for k in range(KT):
                    last = tr(ps[:, tb * 1024 + k * P:tb * 1024 + (k + 1) * P], xn[:, tb * D + k * P:tb * D + (k + 1) * P], ident)
                last.then_inc(sm["h_ps"], 1)
            wa_v = wa[:, :].rearrange("p (s k n) -> p s k n", s=8, k=KT)
            pe.wait_ge(sm["h_ready"], 2)

            def project(n):
                w = a_cols[n][1]
                pe.wait_ge(wa_full[n % 8], 16 * (n // 8 + 1))
                if n >= 2:
                    pe.wait_ge(sm["z_copied"], n - 1)
                for k in range(KT):
                    last = mm(bank(n % 2, 0, T, slice(0, w)), wa_v[:, n % 8, k, 0:w], hv[:, k, :], start=k == 0, stop=k == KT - 1)
                last.then_inc(sm["proj_done"], 1)

            for n in range(3):
                project(n)
            pe.wait_ge(sm["lo_act"], 1)
            for c in range(KT):
                if c >= 2:
                    pe.wait_ge(sm["up_sig"], c - 1)
                for b_, rows in ((2, slice(0, LORA)), (3, slice(LORA, P))):
                    last = mm(bank(b_ + 2 * (c % 2), 0, T), upw[rows, c * P:(c + 1) * P], zs[0][0][rows, :], start=True, stop=True)
                last.then_inc(sm["up_done"], 1)
            pe.wait_ge(sm["up_sig"], KT)
            pe.wait_ge(sm["lo_act"], 2)

            def products(c):
                b = c % 2
                pe.wait_ge(sm["feat_ready"], c + 1)
                if c:
                    pe.wait_ge(sm["gram_out"], c)
                for q in range(NCH):
                    for hh in range(2):
                        rows = slice(HD * hh, HD * hh + HD)
                        last = mm(bank(4 + hh, q * P, P), bf[b][rows, q * P:(q + 1) * P], ar[b][rows, q * P:(q + 1) * P], start=True, stop=True)
                last.then_inc(sm["gram_done"], 1)
                if c:
                    pe.wait_ge(sm["tr_out"], c)
                for q in range(NCH):
                    tr(bank(6, q * P, P), bf[b][:, q * P:(q + 1) * P], ident)
                pe.wait_ge(sm["zs_used"], c + 1)
                for tb in range(TB):
                    tr(bank(7, tb * P, P), zs[b][2][:, tb * P:(tb + 1) * P], ident)
                for tb in range(TB):
                    last = mm(bank(3, tb * HEADS + 2 * c, 2), qb[b][:, tb * P:(tb + 1) * P], C("of_head"), start=True, stop=True)
                last.then_inc(sm["tr_done"], 1)

            for c in range(KT):
                for j in range(3):
                    project(3 + 3 * c + j)
                pe.wait_ge(sm["sq_ready"], c + 1)
                mm(bank(2, 0, T), C("headones"), sqb[:, :], start=True, stop=True).then_inc(sm["norm_done"], 1)
                if c:
                    products(c - 1)
            products(KT - 1)
            meet(pe, 1)
            pe.wait_ge(sm["ws_in"], 16)
            for g in range(GROUPS):
                last = tr(ps[:, 4 * 512 + g * P:4 * 512 + (g + 1) * P], wsr[:, g * P:(g + 1) * P], ident)
            last.then_inc(sm["wst_ps"], 1)
            wb_v = wb[:, :].rearrange("p (s k n) -> p s k n", s=2, k=KT)

            def chunk(n, lhs, free, b0=None):
                pe.wait_ge(wb_full[n % 2], 16 * (n // 2 + 1))
                for tb in range(TB):
                    m_ = 2 * n + tb
                    free(m_)
                    for k in range(KT):
                        last = mm(bank(m_ % 4), lhs[:, k, tb * P:(tb + 1) * P], wb_v[:, n % 2, k, :], start=k == 0, stop=k == KT - 1)
                    last.then_inc(sm["pb_done"], 1)

            def out_free(m_):
                if m_ >= 12:
                    pe.wait_ge(sm["gate_pre"], m_ - 12 + 1)
                elif m_ >= 4:
                    pe.wait_ge(sm["pb_out"], m_ - 4 + 1)
            for n in range(4):
                chunk(n, hv, out_free)
            for n in range(4, 6):
                chunk(n, hv, out_free)
            pe.wait_ge(sm["wst_ready"], 1)
            for tb in range(TB):
                pe.wait_ge(sm["vn_ready"], tb + 1)
                if tb:
                    pe.wait_ge(sm["sp_out"], tb)
                for g in range(GROUPS):
                    last = mm(ps[:, 6 * 512 + g * P:6 * 512 + (g + 1) * P], wst[:, g * P:(g + 1) * P],
                              vsb[:, tb * D + g * P:tb * D + (g + 1) * P], start=True, stop=True)
                last.then_inc(sm["sp_done"], 1)
            for n in range(6, 8):
                chunk(n, hv, out_free)
            pe.wait_ge(sm["x1_ready"], 1)
            gup_q = gup[:, :].rearrange("s (q t) -> s q t", q=PAIRS)
            for r in range(4):
                if r:
                    pe.wait_ge(sm["x21_out"], r)
                for q in range(16):
                    pr = 16 * r + q
                    last = mm(bank(4, 32 * q, 32, slice(32, 64)), gup_q[0:32, pr, 32:64], x1w[0:32, pr * 32:(pr + 1) * 32], start=True, stop=True)
                last.then_inc(sm["w1_done"], 1)
                pe.wait_ge(sm["w1_out"], r + 1)
                for q in range(16):
                    pr = 16 * r + q
                    last = mm(bank(5, 32 * q, 32, slice(0, 32)), x1w[32:64, pr * 32:(pr + 1) * 32], gup_q[32:64, pr, 32:64], start=True, stop=True)
                last.then_inc(sm["x21_done"], 1)
            meet(pe, 2)
            pe.wait_ge(sm["v_put"], NCH)
            for c in range(NCH):
                y0 = CH * (c % 2)
                for g in range(2):
                    pe.wait_ge(sm["s_out"], 2 * c + g + 1)
                    if c:
                        pe.wait_ge(sm["r_out"], 2 * (c - 1) + g + 1)
                    for i in range(8):
                        h = 8 * g + i
                        q = h * NCH + c
                        last = mm(bank(g, i * HD, HD, slice(0, CH)), arg[:, q * P:q * P + CH], zst[:, c * D + h * HD:c * D + (h + 1) * HD], start=True, stop=True)
                    last.then_inc(sm["r_done"], 1)
                for g in range(2):
                    pe.wait_ge(sm["r_out"], 2 * c + g + 1)
                    if c:
                        pe.wait_ge(sm["u_out"], 2 * (c - 1) + g + 1)
                    for i in range(8):
                        h = 8 * g + i
                        q = h * NCH + c
                        last = mm(bank(2 + g, i * HD, HD, slice(0, CH)), gup[:, q * P:q * P + CH], rhs[:, h * HD:(h + 1) * HD], start=True, stop=True)
                    last.then_inc(sm["u_done"], 1)
                pe.wait_ge(sm["uv_v"], c + 1)
                for g in range(2):
                    pe.wait_ge(sm["u_out"], 2 * c + g + 1)
                    if c == NCH - 1:
                        continue
                    if c:
                        pe.wait_ge(sm["s_out"], 2 * c + g + 1)
                    for i in range(8):
                        h = 8 * g + i
                        q = h * NCH + c
                        last = mm(bank(4 + g, i * HD, HD, slice(0, HD)), bk[:, q * HD:(q + 1) * HD], uv[:, h * HD:(h + 1) * HD], start=True, stop=True)
                    last.then_inc(sm["s_done"], 1)
                if c == 2:
                    pe.wait_ge(sm["y_out"], 1)
                for g in range(2):
                    for i in range(8):
                        h = 8 * g + i
                        q = h * NCH + c
                        o = bank(6 + g, i * HD, HD, slice(y0, y0 + CH))
                        mm(o, arg[:, q * P + CH:(q + 1) * P], zst[:, c * D + h * HD:c * D + (h + 1) * HD], start=True, stop=False)
                        last = mm(o, gup[:, q * P + CH:(q + 1) * P], uv[0:CH, h * HD:(h + 1) * HD], start=False, stop=True)
                    last.then_inc(sm["y_done"], 1)
            meet(pe, 3)
            pe.wait_ge(sm["late_in"], 96)
            for tb in range(TB):
                for half in range(2):
                    o = bank(2 * tb + half)
                    mm(o, sg[:, tb * P:(tb + 1) * P], gu1[:, 512 * half:512 * half + 512], start=True, stop=False)
                    last = mm(o, sg[0:32, T + tb * P:T + (tb + 1) * P], gu2[:, 512 * half:512 * half + 512], start=False, stop=True)
                last.then_inc(sm["glora_done"], 1)
            for tb in range(TB):
                pe.wait_ge(sm["m_ready"], tb + 1)
                if tb:
                    pe.wait_ge(sm["mT_ready"], tb)
                for k in range(KT):
                    last = tr(ps[:, 4 * 512 + k * P:4 * 512 + (k + 1) * P], ysb[:, tb * D + k * P:tb * D + (k + 1) * P], ident)
                last.then_inc(sm["m_ps"], 1)
            pe.wait_ge(sm["mT_ready"], 2)
            mv = mT[:, :].rearrange("p (k t) -> p k t", k=KT)
            for n in range(NBC, NBC + 2):
                chunk(n, mv, lambda m_: None)
            for tb in range(TB):
                pe.wait_ge(sm["h2_ready"], tb + 1)
                if tb:
                    pe.wait_ge(sm["mT_ready"], 3)
                for k in range(KT):
                    last = tr(ps[:, 4 * 512 + k * P:4 * 512 + (k + 1) * P], h2[:, tb * D + k * P:tb * D + (k + 1) * P], ident)
                last.then_inc(sm["h2_ps"], 1)
            for tb in range(TB):
                pe.wait_ge(sm["mT_ready"], 2 + tb + 1)
                o = bank(6 * tb, 0, EXPERTS)
                mm(o, C("ones")[0:1, :], br[:, :], start=True, stop=False)
                for k in range(KT):
                    last = mm(o, mv[:, k, tb * P:(tb + 1) * P], wr[:, k * EXPERTS:(k + 1) * EXPERTS], start=False, stop=k == KT - 1)
                last.then_inc(sm["lg_done"], 1)
            pe.wait_ge(sm["mask_ready"], 2)
            m0, m1_ = mask[:, 0:EXPERTS], mask[:, EXPERTS:2 * EXPERTS]
            mm(bank(1, 0, EXPERTS), C("before"), m0, start=True, stop=True)
            mm(bank(1, EXPERTS, EXPERTS), C("before"), m1_, start=True, stop=False)
            mm(bank(1, EXPERTS, EXPERTS), C("ones"), m0, start=False, stop=True)
            mm(bank(1, 128, EXPERTS), C("ones"), m0, start=True, stop=False)
            mm(bank(1, 128, EXPERTS), C("ones"), m1_, start=False, stop=True).then_inc(sm["pos_done"], 1)
            pe.wait_ge(sm["gate_ready"], 2)
            for tb in range(TB):
                last = tr(bank(7, tb * P, P, slice(0, EXPERTS)), gate[:, tb * EXPERTS:(tb + 1) * EXPERTS], ident)
            last.then_inc(sm["gt_ps"], 1)
            pe.wait_ge(sm["gt_ready"], 1)
            for tb in range(TB):
                for half in range(2):
                    last = mm(bank(2 + 2 * tb + half), gt[:, tb * P:(tb + 1) * P], bd[:, 512 * half:512 * half + 512], start=True, stop=True)
            last.then_inc(sm["bd_done"], 1)
            pe.sem_inc(sm["split_used"], NB)
            pe.sem_inc(sm["comb_used"], 1)
            meet(pe, 4)

            def both(o, lhs, rh, rl, start, stop):
                mm(o, lhs, rh, start=start, stop=False)
                return mm(o, lhs, rl, start=False, stop=stop)

            pe.wait_ge(sm["mrg_ready"], 1)
            pe.wait_ge(sm["zeroed"], 3)

            def turn(src):
                mm(bank(6, 0, SLOTS), src[:, 0:P], ident[0:SLOTS, 0:SLOTS], start=True, stop=True)
                for k in range(1, KT):
                    last = tr(bank(6, k * SLOTS, SLOTS), src[:, k * P:(k + 1) * P], ident[0:SLOTS, 0:SLOTS])
                return last

            def step(p, e, s, u):
                slot, fill = ring_at(p, e, s)
                buf = split_buf(e, s, u)
                if s == 0:
                    ne = eno(p, e)
                    pe.wait_ge(sm["gu_read"], ne + 1)
                    pe.wait_ge(sm["xt_lo"], ne + 1)
                if s == KT:
                    pe.wait_ge(sm["at_lo"], eno(p, e))
                    if not (isinstance(e, int) and e == 1):
                        pe.wait_ge(sm["y_lo"], eno(p, e) - 1)
                w_ = ring[:, slot * PIECE:(slot + 1) * PIECE]
                if s in UNSPLIT:
                    pe.wait_ge(ring_full[slot], fill * 16)
                    if s < KT:
                        for q in range(4):
                            w = slice(512 * q, 512 * q + 512)
                            last = mm(ps[0:SLOTS, w], xf[u % 2][:, :], w_[:, w], start=False, stop=False)
                    else:
                        for two in range(2):
                            for half in range(2):
                                w = slice(D * two + 512 * half, D * two + 512 * half + 512)
                                last = mm(bank(4 + half, 0, 512, slice(0, SLOTS)), af[:, two * SLOTS:(two + 1) * SLOTS], w_[:, w], start=False, stop=False)
                    last.then_inc(ring_read[slot], 1)
                    return
                pe.wait_ge(ring_read[slot], fill + 1)
                if s < KT:
                    for q in range(4):
                        w = slice(512 * q, 512 * q + 512)
                        last = both(ps[:, w], xs[u % 2][:, s * S2:(s + 1) * S2], wh[buf][:, w], wl[buf][:, w], s == 0, False)
                        if s == KT - 1:
                            last = mm(ps[SLOTS:P, w], zero[:, 0:SLOTS], zero[:, :], start=False, stop=True)
                else:
                    for two in range(2):
                        f = 2 * (s - KT) + two
                        for half in range(2):
                            w = slice(D * two + 512 * half, D * two + 512 * half + 512)
                            last = both(bank(4 + half), as_[:, f * S2:(f + 1) * S2], wh[buf][:, w], wl[buf][:, w], f == 0, f == KT - 1)
                last.then_inc(sm["split_used"], 1)

            def task(p, e, what, u):
                n = eno(p, e)
                if what in ("sc0", "sc1"):
                    tb = int(what[2])
                    if tb == 0:
                        pe.wait_ge(sm["y_lo"], n - 1)
                    else:
                        pe.wait_ge(sm["sc_added"], 2 * n - 4 + 1 + 1)
                    q = (u - 2) % 4
                    for half in range(2):
                        lt = oht[:, q * T + tb * P:q * T + (tb + 1) * P]
                        mm(bank(6 + half), lt, yh[:, 512 * half:512 * half + 512], start=True, stop=False)
                        last = mm(bank(6 + half), lt, yl[:, 512 * half:512 * half + 512], start=False, stop=True)
                    last.then_inc(sm["sc_done"], 1)
                if what == "low":
                    pe.wait_ge(sm["cb_ready"], n + 1)
                    pe.wait_ge(bias_in, 16 * n + 16)
                    for q in range(4):
                        w = slice(512 * q, 512 * q + 512)
                        last = mm(ps[0:SLOTS, w], mrg[:, :], comb[:, w], start=False, stop=True)
                    last.then_inc(sm["comb_used"], 1)
                if what == "at":
                    pe.wait_ge(sm["act_ready"], n)
                    if not (isinstance(e, int) and e == 1):
                        pe.wait_ge(sm["sc_added"], 2 * n - 4 + 2 + 1)
                    last = turn(acts)
                    last.then_inc(sm["at_done"], 1)
                if what == "ga":
                    if isinstance(e, int) and e < 0:
                        pe.wait_ge(sm["sc_added"], 2 * n + 2 + 1)
                    elif not (isinstance(e, int) and e == 0):
                        pe.wait_ge(sm["at_lo"], n)
                    pe.wait_ge(sm["oh_ready"], n + 2)
                    for half in range(2):
                        for tb in range(TB):
                            for hl, src in enumerate((h2h, h2l)):
                                last = mm(bank(6 + half, 0, 512, slice(0, SLOTS)), oh[:, tb * S2:tb * S2 + SLOTS],
                                          src[:, tb * D + 512 * half:tb * D + 512 * half + 512],
                                          start=tb == 0 and hl == 0, stop=tb == TB - 1 and hl == 1)
                    last.then_inc(sm["ga_done"], 1)
                if what == "xt":
                    pe.wait_ge(sm["xe_ready"], n + 2)
                    turn(xe)
                    for tb in range(TB):
                        tr(bank(7, tb * P, P), oh[:, tb * S2:(tb + 1) * S2].bitcast(fp32), ident)
                    for tb in range(TB):
                        last = mm(bank(7, T, 1), oh[:, tb * S2:(tb + 1) * S2].bitcast(fp32),
                                  col(gate, tb, e + 1), start=tb == 0, stop=tb == 1)
                    last.then_inc(sm["xt_done"], 1)

            moe_steps(pe, step, task, tensor=True)
            meet(pe, 5)


def kernel(**inputs):
    import numpy as _np
    import concourse.bacc as _bacc
    from concourse.bass_utils import run_bass_kernel_spmd as _run

    nc = _bacc.Bacc("TRN2", target_bir_lowering=False, num_devices=1)
    arrays, args = {"cst": constants()}, {}
    for name, a in inputs.items():
        arrays[name] = _np.ascontiguousarray(a)
    for name, a in arrays.items():
        args[name] = nc.dram_tensor(name, a.shape, mybir.dt.from_np(a.dtype), kind="ExternalInput").ap()
    out = nc.dram_tensor("out", (1, T, D), mybir.dt.float32, kind="ExternalOutput").ap()
    build(nc, out=out, **args)
    r = _run(nc, [arrays], core_ids=[0])
    return r.results[0]["out"]
```

```python
import numpy as np
import concourse.bass as bass
from concourse import mybir
from contextlib import ExitStack

T, D = 256, 1024
P = 128
KT = D // P
TB = T // P
HEADS, HD = 16, 64
CH = 64
NCH = T // CH
PAIRS = HEADS * NCH
LORA = 64
GLORA = 160
COLS_A = 3 * D + 2 * LORA + GLORA
GROUPS = 8
EXPERTS, TOPK = 32, 4
FF = D
SLOTS = 64
KAPPA = float(np.exp(-0.5))
RMS_EPS, LN_EPS, GN_EPS = 1e-5, 1e-5, 64e-5
LIMIT, ALPHA = 7.0, 1.702

VEC, VROWS = {}, 0
for _name, _n in (("norm1", KT), ("mix_r", KT), ("mix_k", KT), ("mix_v", KT), ("mix_lora", 3),
                  ("w0", KT), ("a0", KT), ("k_k", KT), ("k_a", KT), ("r_k", KT), ("b_sp", GROUPS)):
    VEC[_name] = (VROWS, _n)
    VROWS += _n

CST, _at = {}, 0
for _name, _n in (("ident", P), ("gmask", P), ("headones", P), ("before", P), ("ones", P), ("causal", P),
                  ("carry", T), ("iota_slot", 2 * SLOTS), ("merge", SLOTS), ("iota_exp", EXPERTS), ("of_head", 2)):
    CST[_name] = (_at, _n)
    _at += _n
CST_W = _at


def constants():
    c = np.zeros((P, CST_W), np.float32)
    p = np.arange(P)[:, None]
    j = np.arange(P)[None, :]

    def put(name, a):
        at, n = CST[name]
        c[:, at:at + n] = a
    put("ident", p == j)
    s, t = p % CH, j % CH
    put("gmask", np.where(j < CH, s < t, s <= t))
    put("headones", p // HD == j // HD)
    put("before", p < j)
    put("ones", 1.0)
    put("causal", p <= j)
    put("carry", (np.arange(T)[None, :] % CH) != 0)
    put("iota_slot", (np.arange(2 * SLOTS) % SLOTS)[None, :])
    put("merge", (p - SLOTS == np.arange(SLOTS)[None, :]) | (p < 2))
    put("iota_exp", np.arange(EXPERTS)[None, :])
    put("of_head", p // HD == np.arange(2)[None, :])
    return c


def build(nc, cst, x, norm1_g, w_in, b_gate, time_mix, w_decay_up, w0, a_up, a0, g_up, k_k, k_a, r_k,
          gn_w, gn_b, ln_v_g, ln_v_b, w_spatial, b_spatial, w_out, norm2_g, w_router, b_router,
          w_gate_up, b_gate_up, w_down, b_down, norm_f_g, out):
    fp32, f32r, i32, u32 = mybir.dt.float32, mybir.dt.float32r, mybir.dt.int32, mybir.dt.uint32
    ALU, ACT, AX = mybir.AluOpType, mybir.ActivationFunctionType, mybir.AxisListType
    V, S, G, E = nc.vector, nc.scalar, nc.gpsimd, nc.tensor
    MUL, ADD, SUB = ALU.mult, ALU.add, ALU.subtract

    ctx = ExitStack()
    with ctx:
        KB = 1024
        BASE = 16512
        TOP = 229344

        def at(name, off, cols, dt=fp32, parts=P):
            assert BASE + off + 4 * cols <= TOP, (name, off, cols)
            return nc.alloc_sbuf_tensor_at(name, [parts, cols], dt, offset=BASE + off)

        class Map:
            def __init__(self, lo, hi):
                self.at, self.hi = lo, hi

            def take(self, name, cols, dt=fp32, parts=P):
                t = at(name, self.at, cols, dt, parts)
                self.at += -(-4 * cols // 32) * 32
                assert self.at <= self.hi, (name, self.at, self.hi)
                return t

        END = TOP - BASE
        keep = Map(0, END)
        cs_ = keep.take("consts", CST_W)
        vec = keep.take("vec", VROWS)
        xacc = keep.take("xacc", TB * D)
        small = keep.take("small", 512)
        WBUF = keep.at
        wa = at("wa", WBUF, 8 * KT * P)
        wb = at("wb", WBUF, 2 * KT * 512)
        bc = at("bc", WBUF + 32 * KB, 4 * D)
        RING, PIECE = 6, 2 * FF
        ring = at("ring", WBUF, RING * PIECE)
        FRONT = WBUF + 48 * KB

        m = Map(FRONT, END)
        hT = m.take("hT", KT * T)
        arg = m.take("arg", PAIRS * P)
        gup = m.take("gup", PAIRS * P, parts=CH)
        bk = m.take("bk", PAIRS * HD)
        vtok = m.take("vtok", TB * D)
        sg = m.take("sg", 2 * T)
        bonus = m.take("bonus", TB * HEADS)
        plast = m.take("plast", PAIRS, parts=CH)
        m1 = Map(m.at, END)
        upw = m1.take("upw", D)
        zp = [[m1.take(f"zp{i}{b}", T + 2) for i in range(3)] for b in range(2)]
        zs = [[m1.take(f"zs{i}{b}", T) for i in range(3)] for b in range(2)]
        qb = [m1.take(f"q{b}", T) for b in range(2)]
        ar = [m1.take(f"ar{b}", 2 * T) for b in range(2)]
        bf = [m1.take(f"bf{b}", 2 * T) for b in range(2)]
        dec, decp, inv, nrm, sqb, tmp, csum, csump, kr, kp = (
            m1.take(n, T) for n in "dec decp inv nrm sqb tmp csum csump kr kp".split())
        sw = at("sw", WBUF + 32 * KB, KT * T)
        sa = at("sa", WBUF + 40 * KB, KT * T)
        xn = at("xn", FRONT + 8 * KB, TB * D)
        xj = at("xj", FRONT + 24 * KB, D)
        vrow = at("vrow", FRONT + 32 * KB, P)
        m2 = Map(m.at, END)
        vsb = m2.take("vsb", TB * D)
        mb = m2.take("mb", TB * D)
        LATE = m2.at
        al = m2.take("al", 1024)
        xl = m2.take("xl", 1024)
        prod = m2.take("prod", 1024)
        x1w = m2.take("x1w", PAIRS * 32, parts=CH)
        wsr = m2.take("wsr", GROUPS * P)
        wst = m2.take("wst", GROUPS * P)
        m3 = Map(LATE, END)
        zst = m3.take("zst", NCH * HEADS * HD)
        uv = m3.take("uv", HEADS * HD)
        rhs = m3.take("rhs", HEADS * HD, parts=CH)
        gu1 = m3.take("gu1", D)
        gu2 = bc[0:32, 3 * D:4 * D]
        yt = zst[:, 0:D]
        ysb = at("ysb", FRONT, TB * D)
        m4 = Map(FRONT + 8 * KB, FRONT + 64 * KB)
        bg = m4.take("bg", 2 * FF, parts=EXPERTS)
        bgh = m4.take("bgh", 2 * FF, f32r, parts=EXPERTS)
        bgl = m4.take("bgl", 2 * FF, f32r, parts=EXPERTS)
        unread = m4.take("unread", D)
        m4 = Map(FRONT + 64 * KB, FRONT + 88 * KB)
        mT = m4.take("mT", KT * T)
        wr = m4.take("wr", KT * EXPERTS)
        br = m4.take("br", EXPERTS, parts=1)
        h2 = m4.take("h2", TB * D)
        lg, el, mask = (m4.take(n, TB * EXPERTS) for n in ("lg", "el", "mask"))
        mx = m4.take("mx", TB * 8)
        ix = m4.take("ix", TB * 8, u32)
        ixf = m4.take("ixf", TB * 8)
        bd = m4.take("bd", D, parts=EXPERTS)
        gt = m4.take("gt", T, parts=EXPERTS)
        NB = 4
        SPLIT = 118 * KB
        m5 = Map(FRONT + SPLIT, END)
        h2h = m5.take("h2h", TB * D, f32r)
        h2l = m5.take("h2l", TB * D, f32r)
        posm = m5.take("posm", TB * EXPERTS)
        gate = m5.take("gate", TB * EXPERTS)
        npass = m5.take("npass", 8, i32)
        gs = m5.take("gs", 8)
        nf = m5.take("nf", D)
        m5 = Map(FRONT, FRONT + SPLIT)
        wh = [m5.take(f"wh{b}", PIECE, f32r) for b in range(NB)]
        wl = [m5.take(f"wl{b}", PIECE, f32r) for b in range(NB)]
        S2 = 2 * SLOTS
        oh = m5.take("oh", TB * S2, f32r)
        oht = m5.take("oht", 4 * T, f32r)
        xe = m5.take("xe", D, parts=SLOTS)
        xs = [m5.take(f"xs{b}", KT * S2, f32r) for b in range(2)]
        xf = [m5.take(f"xf{b}", SLOTS) for b in range(2)]
        gc = m5.take("gc", FF, parts=SLOTS)
        uc = m5.take("uc", FF, parts=SLOTS)
        sgm = m5.take("sgm", FF, parts=SLOTS)
        acts = gc
        as_ = m5.take("as", KT * S2, f32r)
        af = m5.take("af", 2 * SLOTS)
        yh = m5.take("yh", D, f32r)
        yl = m5.take("yl", D, f32r)
        comb = m5.take("comb", 2 * FF, f32r)
        mrg = m5.take("mrg", SLOTS, f32r)
        zero = nc.alloc_sbuf_tensor_at("zero", [1, 512], mybir.dt.bfloat16, offset=BASE + m5.at)
        m5.at += KB

        def C(name, rows=slice(0, P)):
            a, n = CST[name]
            return cs_[rows, a:a + n]

        def vcol(name, i=0):
            return vec[:, VEC[name][0] + i:VEC[name][0] + i + 1]

        scr_a = nc.dram_tensor("scr_a", [P, 32, 32], fp32).ap()
        scr_x = nc.dram_tensor("scr_x", [P, 32, 32], fp32).ap()
        scr_b = nc.dram_tensor("scr_b", [EXPERTS, 2, 2 * FF], f32r).ap()

        ps = ctx.enter_context(nc.psum_tensor("ps", [P, 8 * 512], fp32))

        def bank(b, lo=0, n=512, parts=slice(0, P)):
            return ps[parts, 512 * b + lo:512 * b + lo + n]

        def sem(name):
            return ctx.enter_context(nc.semaphore(name))

        stage_end = {k: sem(f"stage_end{k}") for k in (1, 2)}
        misc = [sem(f"misc_loaded{i}") for i in range(2)]
        x_in = sem("x_in")
        wa_full = [sem(f"wa_full{i}") for i in range(8)]
        wb_full = [sem(f"wb_full{i}") for i in range(2)]
        dve_chain, act_chain = sem("dve_chain"), sem("act_chain")
        names = ("act_ready arg_top at_done at_hi at_lo b_hi b_split b_st bc_in bd_done comb_used cb_ready csum_ready dec_ready "
                 "e_out eps_ready feat_ready fin_ready ga_done gate_pre gate_ready gate_sig gc_ready "
                 "glora_done glora_out gn_sqrt gram_done gram_out gt_ps gt_ready gu_read mrg_ready  h2_hi h2_ps h2_ready "
                 "h_ps h_ready hi_ready lanes_done lanes_ld lanes_st late_in gu_in lg_done ln_mean ln_sq ln_sqrt lo_act "
                 "lo_mixed mT_ready m_ps m_ready mask_ready neg_max nf_in norm_done nrm_ready o_out oh_ready "
                 "pads pb_done pb_out split_used pos_done pos_moved npass_ready proj_done q_ready r_done r_out s_done "
                 "s_out sc_added sc_done sig_done sp_done sp_out sq_ready stored sumsq tr_done tr_out u_done u_out "
                 "ug_ready up_done up_sig uv_v v_put vec_ps vec_ready vn_ready w1_done w1_out ws_in wst_copied wst_ps "
                 "wst_ready upw_in rows_in x1_ready x21_done x21_out x_st zeroed xe_ready xn_ready xrms xt_done xt_hi "
                 "xt_in xt_lo y_done y_hi y_lo y_out yc_ready yc_sq yvar z_copied zk_ready zr_ready zs_used").split()
        sm = {n: sem(n) for n in names}
        bias_in = sem("bias_in")
        ring_full = [sem(f"ring_full{i}") for i in range(RING)]
        ring_read = [sem(f"ring_read{i}") for i in range(RING)]

        class Chain:
            def __init__(self, eng, s):
                self.eng, self.s, self.n = eng, s, 0

            def __call__(self, ins):
                self.n += 1
                ins.then_inc(self.s, 1)
                self.eng.wait_ge(self.s, self.n)

        class Own:
            def __init__(self, eng):
                self.eng, self.n = eng, {}

            def __call__(self, name):
                self.n[name] = self.n.get(name, 0) + 1
                self.eng.wait_ge(sm[name], self.n[name])

        def meet(eng, k):
            eng.drain().then_inc(stage_end[k], 1)
            eng.wait_ge(stage_end[k], 4)

        block = ctx.enter_context(nc.Block())

        a_cols = [(3 * D, P), (3 * D + P, P), (3 * D + 2 * P, 32)]
        for c in range(KT):
            a_cols += [(D + c * P, P), (c * P, P), (2 * D + c * P, P)]
        NA = len(a_cols)
        b_cols = [COLS_A + D, COLS_A + D + 512, COLS_A, COLS_A + 512,
                  COLS_A + 3 * D, COLS_A + 3 * D + 512, COLS_A + 2 * D, COLS_A + 2 * D + 512]
        NBC = len(b_cols)

        UNSPLIT = (2, 10)
        GU_UNSPLIT, DOWN_UNSPLIT = UNSPLIT
        PER_PASS = EXPERTS * 12
        SPLITS = 12 - len(UNSPLIT)
        GU_SPLITS = KT - 1

        def passes(eng):
            return eng.value_load(npass[0:1, 0:1], min_val=1, max_val=T // SLOTS)

        def eno(p, e):
            return p * EXPERTS + e

        def ring_at(p, e, s):
            edge = isinstance(e, int)
            o = s if edge and e == 0 else s - 12 if edge and e == EXPERTS else s - 4
            return o % RING, p * (PER_PASS // RING) + 2 * e + (o // RING + 1)

        def split_no(p, e, s):
            before = sum(1 for i in range(s) if i not in UNSPLIT)
            edge = isinstance(e, int)
            o = before if edge and e == 0 else before - SPLITS if edge and e == EXPERTS else before + GU_SPLITS - SPLITS
            return p * (EXPERTS * SPLITS) + SPLITS * e + o

        def split_buf(e, s, u):
            return split_no(0, e if isinstance(e, int) else 4 + u, s) % NB

        def last_gu(p, e):
            return split_no(p, e, KT - 1) + 1

        def last_down(p, e):
            return split_no(p, e + 1, 11) + 1

        def col(t, tb, e):
            return t[:, bass.ds(tb * EXPERTS + e, 1)] if not isinstance(e, int) else t[:, tb * EXPERTS + e:tb * EXPERTS + e + 1]

        def scatter_bank(e, tb):
            return 0 if isinstance(e, int) and e == EXPERTS + 1 and tb == 1 else 6

        PLAN_ACT = {1: ["y"], 5: ["at"], 6: ["ga"], 8: ["xt"], 10: ["low"], 11: ["glu"]}
        PLAN_DVE = {0: ["oh"], 1: ["y", "act"], 3: ["sc0"], 4: ["sc1"], 5: ["at"], 8: ["xt"], 10: ["glu"]}
        PLAN_PE = {1: ["sc0"], 2: ["sc1"], 3: ["at"], 4: ["ga"], 6: ["xt"], 8: ["low"]}
        RUNS = {"oh": (0, EXPERTS - 2), "ga": (0, EXPERTS - 2), "xt": (0, EXPERTS - 2),
                "low": (0, EXPERTS - 1), "glu": (0, EXPERTS - 1),
                "act": (1, EXPERTS), "at": (1, EXPERTS),
                "y": (2, EXPERTS + 1), "sc0": (2, EXPERTS + 1), "sc1": (2, EXPERTS + 1)}

        def iteration(p, e, u, like, step, task, plan, done=0):
            for s in range(12):
                if s >= done and (like < EXPERTS if s < KT else 1 <= like <= EXPERTS):
                    step(p, e, s, u)
                for what in plan.get(s, ()):
                    if RUNS[what][0] <= like <= RUNS[what][1]:
                        task(p, e, what, u)

        BEGIN_PE = (("task", "ga"), ("task", "xt"))
        BEGIN_ACT = (("step", 0), ("task", "ga"), ("task", "xt"))
        BEGIN_DVE = (("task", "oh"), ("step", 0), ("task", "xt"))
        FIRST_PE = {8: ["ga", "low", "xt"]}
        FIRST_ACT = {8: ["low", "ga", "glu", "xt"]}
        FIRST_DVE = {0: ["oh"], 8: ["glu", "xt"]}
        LAST_PE = {0: ["at"], 9: ["sc0"], 10: ["sc1"]}
        LAST_ACT = {8: ["at", "y"]}
        LAST_DVE = {0: ["act"], 8: ["at", "y"], 10: ["sc0"], 11: ["sc1"]}

        def moe_steps(eng, step, task, begin, first, plan, last):
            with eng.Fori(0, passes(eng)) as p:
                done = 0
                for kind, what in begin:
                    if kind == "step":
                        step(p, 0, what, 0)
                        done = what + 1
                    else:
                        task(p, -1, what, 3)
                iteration(p, 0, 0, 0, step, task, first, done)
                iteration(p, 1, 1, 1, step, task, plan)
                with eng.Fori(0, EXPERTS // 4 - 1) as i:
                    for v in range(4):
                        iteration(p, i * 4 + (2 + v), (2 + v) % 4, 2, step, task, plan)
                for e in range(EXPERTS - 2, EXPERTS + 2):
                    iteration(p, e, e % 4, e, step, task, last if e == EXPERTS else plan)
                if plan is PLAN_DVE:
                    task(p, EXPERTS + 1, "next", 0)

        @block.sync
        def _(sp):
            w_in_v = w_in[0].rearrange("(k p) n -> p k n", p=P)
            wa_v = wa[:, :].rearrange("p (s k n) -> p s k n", s=8, k=KT)
            wb_v = wb[:, :].rearrange("p (s k n) -> p s k n", s=2, k=KT)
            sp.dma_start(xacc[:, 0:D], x[0, 0:P, :]).then_inc(x_in, 16)
            sp.dma_start(xacc[:, D:2 * D], x[0, P:T, :]).then_inc(x_in, 16)
            sp.dma_start(cs_[:, :], cst).then_inc(misc[0], 16)
            sp.wait_ge(sm["zeroed"], 1)
            for name, src, n in (("w0", w0[0], KT), ("a0", a0[0], KT), ("k_k", k_k[0], KT), ("k_a", k_a[0], KT), ("r_k", r_k[0], KT)):
                r = VEC[name][0]
                sp.dma_start(vrow[r:r + n, :], src.rearrange("(r p) -> r p", p=P)).then_inc(sm["rows_in"], 16)
            r = VEC["b_sp"][0]
            sp.dma_start(vrow[r:r + GROUPS, :], b_spatial[0]).then_inc(sm["rows_in"], 16)
            for n, (c0, w) in enumerate(a_cols):
                if n >= 8:
                    sp.wait_ge(sm["proj_done"], n - 7)
                sp.dma_start(wa_v[:, n % 8, :, 0:w], w_in_v[:, :, c0:c0 + w]).then_inc(wa_full[n % 8], 16)
            w_out_v = w_out[0].rearrange("(k p) n -> p k n", p=P)
            for n in range(NBC + 2):
                if n == 0:
                    sp.wait_ge(sm["proj_done"], NA - NA % 8)
                elif n == 1:
                    sp.wait_ge(sm["proj_done"], NA)
                else:
                    sp.wait_ge(sm["pb_done"], 2 * (n - 1))
                src = w_in_v[:, :, b_cols[n]:b_cols[n] + 512] if n < NBC else w_out_v[:, :, 512 * (n - NBC):512 * (n - NBC + 1)]
                sp.dma_start(wb_v[:, (n + 1) % 2, :, :], src).then_inc(wb_full[n % 2], 16)
            gu_v = w_gate_up[0].rearrange("e (k p) n -> e k p n", p=P)
            dn_v = w_down[0].rearrange("e (j two p) n -> e j p two n", p=P, two=2)

            def load(slot, src):
                sp.dma_start(ring[:, slot * PIECE:(slot + 1) * PIECE].rearrange("p (a n) -> p a n", a=src.shape[1]), src).then_inc(ring_full[slot], 16)

            def gate_up(e, k):
                return gu_v[bass.ds(e, 1), k, :, :].rearrange("e p n -> p e n")

            sp.wait_ge(sm["m_ready"], 2)
            load(4, gate_up(0, 4))
            sp.wait_ge(sm["pb_done"], 2 * NBC + 3)
            load(2, gate_up(0, 2))
            load(3, gate_up(0, 3))
            sp.wait_ge(sm["pb_done"], 2 * NBC + 4)
            load(0, gate_up(0, 0))
            load(1, gate_up(0, 1))
            sp.wait_ge(sm["h2_ready"], 2)
            load(5, gate_up(0, 5))
            sp.wait_ge(sm["npass_ready"], 1)

            def fetch(p, e, s, src):
                slot, fill = ring_at(p, e, s)
                sp.wait_ge(ring_read[slot], fill)
                load(slot, src)

            def weights(p, e, gu=range(KT), down=True):
                for k in gu:
                    fetch(p, e, k, gate_up(e, k))
                if down:
                    for j in range(4):
                        fetch(p, e, KT + j, dn_v[bass.ds(e - 1, 1), j, :, :, :].rearrange("e p two n -> p (e two) n"))

            def pass_weights(p, gu=range(KT)):
                weights(p, 0, gu, down=False)
                with sp.Fori(1, EXPERTS) as e:
                    weights(p, e)
                weights(p, EXPERTS, (), down=True)

            pass_weights(0, range(RING, KT))
            with sp.register("more_passes") as count:
                sp.reg_load(count, npass[0:1, 0:1])
                with sp.If_ne(count, 1):
                    with sp.Fori(1, passes(sp)) as p:
                        pass_weights(p)
            for tb in range(TB):
                sp.wait_ge(sm["fin_ready"], tb + 1)
                sp.dma_start(out[0, tb * P:(tb + 1) * P, :], xacc[:, tb * D:(tb + 1) * D]).then_inc(sm["stored"], 16)
            sp.wait_ge(sm["stored"], 32)

        @block.gpsimd
        def _(pool):
            nc.gpsimd.memset(vrow[0:VROWS, :], 0.0).then_inc(sm["zeroed"], 1)
            pool.wait_ge(sm["zeroed"], 1)

            def rows(name, src, n):
                r = VEC[name][0]
                pool.dma_start(vrow[r:r + n, :], src.rearrange("(r p) -> r p", p=P)).then_inc(misc[1], 16)
            rows("norm1", norm1_g[0], KT)
            rows("mix_r", time_mix[0, 0:D], KT)
            rows("mix_k", time_mix[0, D:2 * D], KT)
            rows("mix_v", time_mix[0, 2 * D:3 * D], KT)
            rows("mix_lora", time_mix[0, 3 * D:3 * D + 2 * P], 2)
            r = VEC["mix_lora"][0] + 2
            pool.dma_start(vrow[r:r + 1, 0:32], time_mix[0:1, 3 * D + 2 * P:COLS_A]).then_inc(misc[1], 16)
            pool.dma_start(upw[0:LORA, :], w_decay_up[0]).then_inc(sm["upw_in"], 16)
            pool.dma_start(upw[LORA:P, :], a_up[0]).then_inc(sm["upw_in"], 16)
            meet(pool, 1)
            gup_v = gup[:, :].rearrange("s (q t) -> s q t", q=PAIRS)
            for half in range(2):
                h = slice(32 * half, 32 * half + 32)
                pool.dma_start(scr_a[half * PAIRS:(half + 1) * PAIRS].rearrange("l s t -> s l t"),
                               gup_v[h, :, h]).then_inc(sm["lanes_st"], 16)
            pool.wait_ge(sm["lanes_st"], 32)
            pool.dma_start(al[:, :], scr_a.rearrange("l s t -> l (s t)")).then_inc(sm["lanes_ld"], 16)
            pool.dma_start(wsr[:, :].rearrange("i (g j) -> i g j", g=GROUPS),
                           w_spatial[0].rearrange("g i j -> i g j")).then_inc(sm["ws_in"], 16)
            for i, src in enumerate((ln_v_g[0], ln_v_b[0], b_gate[0, 0:D], b_gate[0, D:2 * D])):
                pool.dma_start(bc[:, i * D:(i + 1) * D], src.partition_broadcast(P)).then_inc(sm["bc_in"], 16)
            pool.wait_ge(sm["lanes_done"], 1)
            pool.dma_start(scr_x.rearrange("l s t -> l (s t)"), xl[:, :]).then_inc(sm["x_st"], 16)
            pool.wait_ge(sm["x_st"], 16)
            for half in range(2):
                h = slice(32 * half, 32 * half + 32)
                pool.dma_start(gup_v[h, :, h], scr_x[half * PAIRS:(half + 1) * PAIRS].rearrange("l s t -> s l t")).then_inc(sm["xt_in"], 16)
            meet(pool, 2)
            for i, src in enumerate((gn_w[0], gn_b[0], norm2_g[0])):
                pool.dma_start(bc[:, i * D:(i + 1) * D], src.partition_broadcast(P)).then_inc(sm["bc_in"], 16)
            pool.dma_start(gu1[:, :], g_up[0, 0:P, :]).then_inc(sm["gu_in"], 16)
            pool.dma_start(gu2, g_up[0, P:GLORA, :]).then_inc(sm["gu_in"], 16)
            pool.wait_ge(sm["y_done"], 2 * NCH)
            pool.dma_start(wr[:, :].rearrange("p (k n) -> p k n", k=KT),
                           w_router[0].rearrange("(k p) n -> p k n", p=P)).then_inc(sm["late_in"], 16)
            pool.dma_start(br[:, :], b_router).then_inc(sm["late_in"], 16)
            pool.dma_start(bd[:, :], b_down[0]).then_inc(sm["late_in"], 16)
            pool.dma_start(bg[:, :], b_gate_up[0]).then_inc(sm["late_in"], 16)
            pool.wait_ge(sm["b_split"], 1)
            pool.dma_start(scr_b[:, 0, :], bgh[:, :]).then_inc(sm["b_st"], 16)
            pool.dma_start(scr_b[:, 1, :], bgl[:, :]).then_inc(sm["b_st"], 16)
            pool.wait_ge(sm["b_st"], 32)
            pool.wait_ge(sm["m_ready"], 2)
            nc.gpsimd.memset(zero[:, :], 0.0).then_inc(sm["zeroed"], 1)
            nc.gpsimd.memset(comb[0:SLOTS, :].bitcast(fp32), 0.0).then_inc(sm["zeroed"], 1)
            pool.dma_start(nf[:, :], norm_f_g.partition_broadcast(P)).then_inc(sm["nf_in"], 16)
            pool.wait_ge(sm["zeroed"], 3)

            def bias(p, e):
                pool.wait_ge(sm["comb_used"], eno(p, e) + 1)
                pool.dma_start(comb[0:2, :], scr_b[bass.ds(e, 1), :, :].rearrange("e two n -> (e two) n")).then_inc(bias_in, 16)

            pool.wait_ge(sm["npass_ready"], 1)
            with pool.Fori(0, passes(pool)) as p:
                with pool.Fori(0, EXPERTS) as e:
                    bias(p, e)

        @block.scalar
        def _(act):
            act_ = S.activation
            link, own = Chain(act, act_chain), Own(act)
            act.wait_ge(sm["eps_ready"], 1)
            act_(small[:, 63:64], small[:, 60:61], ACT.Sqrt).then_inc(sm["xrms"], 1)
            own("xrms")
            act.wait_ge(x_in, 32)
            for tb in range(TB):
                if tb:
                    act.wait_ge(sm["sumsq"], tb)
                act_(xj[:, :], xacc[:, tb * D:(tb + 1) * D], ACT.Square, accum_out=small[:, tb:tb + 1]).then_inc(sm["sumsq"], 1)
                own("sumsq")
            act.wait_ge(sm["sumsq"], 2)
            act.wait_ge(misc[0], 16)
            act_(small[:, 2:4], small[:, 0:2], ACT.Sqrt, scale=1.0 / D, bias=small[:, 60:61]).then_inc(sm["xrms"], 1)
            own("xrms")
            n_z = [0]

            def zcopy(dst, rows=P):
                n = n_z[0]
                act.wait_ge(sm["proj_done"], n + 1)
                act_(dst[0:rows, 1:T + 1], bank(n % 2, 0, T, slice(0, rows)), ACT.Copy).then_inc(sm["z_copied"], 1)
                own("z_copied")
                n_z[0] += 1

            act.wait_ge(sm["pads"], 1)
            for i in range(3):
                zcopy(zp[0][i], 32 if i == 2 else P)
            act.wait_ge(sm["lo_mixed"], 1)
            act_(zs[0][0][0:LORA, :], zs[0][0][0:LORA, :], ACT.Tanh).then_inc(sm["lo_act"], 1)
            own("lo_act")
            act.wait_ge(sm["lo_mixed"], 3)
            link(act_(sg[:, 0:T], zs[0][1][:, :], ACT.Sigmoid))
            act_(sg[0:32, T:2 * T], zs[0][2][0:32, :], ACT.Sigmoid).then_inc(sm["lo_act"], 1)
            own("lo_act")
            for c in range(KT):
                act.wait_ge(sm["up_done"], c + 1)
                cols = slice(c * T, (c + 1) * T)
                link(act_(sw[:, cols], bank(2 + 2 * (c % 2), 0, T), ACT.Sigmoid, bias=vcol("w0", c)))
                act_(sa[:, cols], bank(3 + 2 * (c % 2), 0, T), ACT.Sigmoid, bias=vcol("a0", c)).then_inc(sm["up_sig"], 1)
                own("up_sig")

            def tile_copies(c):
                b = c % 2
                act.wait_ge(sm["feat_ready"], c + 1)
                for hh in range(2):
                    rows = slice(HD * hh, HD * hh + HD)
                    q0 = (2 * c + hh) * NCH
                    link(act_(arg[0:HD, q0 * P:(q0 + NCH) * P], ar[b][rows, :], ACT.Copy))
                    act_(plast[0:HD, q0:q0 + NCH], dec[rows, CH - 1:T:CH], ACT.Copy).then_inc(sm["arg_top"], 1)
                    own("arg_top")
                act.wait_ge(sm["tr_done"], c + 1)
                for hh in range(2):
                    q0 = (2 * c + hh) * NCH
                    link(act_(bk[:, q0 * HD:(q0 + NCH) * HD].rearrange("p (q j) -> p q j", q=NCH),
                         bank(6).rearrange("p (q h j) -> p q h j", q=NCH, h=2)[:, :, hh, :], ACT.Copy))
                act_(vtok[:, :].rearrange("p (b n) -> p b n", b=TB)[:, :, c * P:(c + 1) * P],
                     bank(7, 0, 2 * P).rearrange("p (b n) -> p b n", b=TB), ACT.Copy).then_inc(sm["tr_out"], 1)
                own("tr_out")

            for c in range(KT):
                b = c % 2
                if c >= 2:
                    act.wait_ge(sm["zs_used"], c - 1)
                zcopy(zp[b][1])
                zcopy(zp[b][0])
                act.wait_ge(sm["zk_ready"], c + 1)
                act_(sqb[:, :], zs[b][1][:, :], ACT.Square, scale=vcol("k_k", c)).then_inc(sm["sq_ready"], 1)
                own("sq_ready")
                zcopy(zp[b][2])
                act.wait_ge(sm["norm_done"], c + 1)
                act_(nrm[:, :], bank(2, 0, T), ACT.Sqrt).then_inc(sm["nrm_ready"], 1)
                own("nrm_ready")
                if c:
                    tile_copies(c - 1)
                act.wait_ge(sm["csum_ready"], c + 1)
                link(act_(dec[:, :], csum[:, :], ACT.Exp, scale=-KAPPA))
                link(act_(decp[:, :], csump[:, :], ACT.Exp, scale=-KAPPA))
                act_(inv[:, :], csum[:, :], ACT.Exp, scale=KAPPA).then_inc(sm["dec_ready"], 1)
                own("dec_ready")
            tile_copies(KT - 1)
            link(act_(bonus[:, :], bank(3, 0, TB * HEADS), ACT.Copy))
            meet(act, 1)
            for n in range(4):
                for tb in range(TB):
                    m_ = 2 * n + tb
                    act.wait_ge(sm["pb_done"], m_ + 1)
                    dst = (vsb if n < 2 else mb)[:, tb * D + 512 * (n % 2):tb * D + 512 * (n % 2) + 512]
                    act_(dst, bank(m_ % 4), ACT.Gelu).then_inc(sm["pb_out"], 1)
                    own("pb_out")
                if n == 1:
                    act.wait_ge(sm["wst_ps"], 1)
                    act_(wst[:, :], ps[:, 4 * 512:6 * 512], ACT.Copy).then_inc(sm["wst_copied"], 1)
                    own("wst_copied")
            for tb in range(TB):
                act.wait_ge(sm["ln_mean"], tb + 1)
                act_(al[:, :], vsb[:, tb * D:(tb + 1) * D], ACT.Square, accum_out=small[:, 10 + tb:11 + tb]).then_inc(sm["ln_sq"], 1)
                own("ln_sq")
            act_(small[:, 12:14], small[:, 10:12], ACT.Sqrt, scale=1.0 / D, bias=small[:, 61:62]).then_inc(sm["ln_sqrt"], 1)
            own("ln_sqrt")
            def x22_rows(r):
                act.wait_ge(sm["w1_done"], r + 1)
                act_(x1w[32:64, r * 512:(r + 1) * 512], bank(4, 0, 512, slice(32, 64)), ACT.Copy).then_inc(sm["w1_out"], 1)
                own("w1_out")

            def gate_sigmoid(n, tb):
                m_ = 2 * (n - 4) + tb
                act.wait_ge(sm["gate_pre"], m_ + 1)
                o = (prod[:, (m_ % 2) * 512:(m_ % 2) * 512 + 512] if n < 6
                     else vsb[:, tb * D + 512 * (n % 2):tb * D + 512 * (n % 2) + 512])
                act_(o, o, ACT.Sigmoid).then_inc(sm["gate_sig"], 1)
                own("gate_sig")

            for r in range(4):
                gate_sigmoid(4 + r // 2, r % 2)
            for r in range(4):
                x22_rows(r)
                gate_sigmoid(6 + r // 2, r % 2)
            meet(act, 2)
            vt_odd = vtok[:, :].rearrange("p (b n) -> p b n", b=TB)
            def put_v(c):
                rows = slice(CH * (c % 2), CH * (c % 2) + CH)
                act_(zst[CH:P, c * D:(c + 1) * D], vt_odd[rows, c // 2, :], ACT.Copy).then_inc(sm["v_put"], 1)
                own("v_put")

            put_v(0)

            def gn_square(tb):
                act.wait_ge(sm["yc_ready"], tb + 1)
                act_(yt, ysb[:, tb * D:(tb + 1) * D], ACT.Square).then_inc(sm["yc_sq"], 1)
                own("yc_sq")

            def gn_root(tb):
                act.wait_ge(sm["yvar"], tb + 1)
                act_(small[:, 80 + 16 * tb:96 + 16 * tb], small[:, 112 + 16 * tb:128 + 16 * tb], ACT.Sqrt, scale=1.0 / HD, bias=small[:, 62:63]).then_inc(sm["gn_sqrt"], 1)
                own("gn_sqrt")

            for c in range(NCH):
                for g in range(2):
                    act.wait_ge(sm["r_done"], 2 * c + g + 1)
                    act_(rhs[:, g * 512:(g + 1) * 512], bank(g, 0, 512, slice(0, CH)), ACT.Copy).then_inc(sm["r_out"], 1)
                    own("r_out")
                if c:
                    act.wait_ge(sm["y_done"], 2 * c)
                act_(uv[CH:P, :], zst[CH:P, c * D:(c + 1) * D], ACT.Copy).then_inc(sm["uv_v"], 1)
                own("uv_v")
                if c == 0:
                    put_v(1)
                if c == 1:
                    put_v(2)
                    put_v(3)
                if c == 2:
                    gn_square(0)
                if c == 3:
                    gn_root(0)
                if c % 2:
                    act.wait_ge(sm["y_done"], 2 * c + 2)
                    act_(ysb[:, (c // 2) * D:(c // 2 + 1) * D], ps[:, 6 * 512:8 * 512], ACT.Copy).then_inc(sm["y_out"], 1)
                    own("y_out")
            def turned(tb, src_ready):
                act.wait_ge(sm[src_ready], tb + 1)
                act_(mT[:, :].rearrange("p (k t) -> p k t", k=KT)[:, :, tb * P:(tb + 1) * P],
                     ps[:, 4 * 512:6 * 512].rearrange("p (k t) -> p k t", k=KT), ACT.Copy).then_inc(sm["mT_ready"], 1)
                own("mT_ready")

            def x2_root(tb):
                act.wait_ge(sm["o_out"], 2 * tb + 2)
                act_(unread[:, :], xacc[:, tb * D:(tb + 1) * D], ACT.Square, accum_out=small[:, 20 + tb:21 + tb]).then_inc(sm["sumsq"], 1)
                own("sumsq")
                act_(small[:, 22 + tb:23 + tb], small[:, 20 + tb:21 + tb], ACT.Sqrt, scale=1.0 / D, bias=small[:, 60:61]).then_inc(sm["xrms"], 1)
                own("xrms")

            def h2_high(tb):
                act_(h2h[:, tb * D:(tb + 1) * D], h2[:, tb * D:(tb + 1) * D], ACT.Copy).then_inc(sm["h2_hi"], 1)
                own("h2_hi")

            def exponent(tb):
                act.wait_ge(sm["neg_max"], tb + 1)
                e_ = slice(tb * EXPERTS, (tb + 1) * EXPERTS)
                act_(el[:, e_], lg[:, e_], ACT.Exp, bias=small[:, 30 + tb:31 + tb]).then_inc(sm["e_out"], 1)
                own("e_out")

            turned(0, "m_ps")
            gn_square(1)
            gn_root(1)
            act.wait_ge(sm["late_in"], 64)
            act_(bgh[:, :], bg[:, :], ACT.Copy).then_inc(sm["b_hi"], 1)
            own("b_hi")
            turned(1, "m_ps")
            x2_root(0)
            turned(0, "h2_ps")
            h2_high(0)
            x2_root(1)
            exponent(0)
            turned(1, "h2_ps")
            h2_high(1)
            exponent(1)

            act_(mrg[:, :], C("merge"), ACT.Copy).then_inc(sm["mrg_ready"], 1)
            halves = lambda t: t[:, :].rearrange("p (k two s) -> p k two s", k=KT, two=2)
            tiles = lambda a: a.rearrange("p (k s) -> p k s", k=KT)

            def hi(p, e, s, u):
                if s in UNSPLIT:
                    return
                slot, fill = ring_at(p, e, s)
                buf = split_buf(e, s, u)
                act.wait_ge(ring_full[slot], fill * 16)
                act.wait_ge(sm["split_used"], split_no(p, e, s) + 1)
                act_(wh[buf][:, :], ring[:, slot * PIECE:(slot + 1) * PIECE], ACT.Copy).then_inc(sm["hi_ready"], 1)

            def task(p, e, what, u):
                if what == "y":
                    act.wait_ge(sm["split_used"], last_down(p, e - 2) + NB)
                    act_(yh[:, :], ps[:, 4 * 512:6 * 512], ACT.Copy, scale=gs[:, (u - 2) % 4:(u - 2) % 4 + 1]).then_inc(sm["y_hi"], 1)
                if what == "at":
                    act.wait_ge(sm["at_done"], eno(p, e))
                    f0 = 2 * (DOWN_UNSPLIT - KT)
                    act_(af[:, :], bank(6, f0 * SLOTS, 2 * SLOTS), ACT.Copy)
                    act_(halves(as_)[:, :, 0, :], tiles(bank(6)), ACT.Copy).then_inc(sm["at_hi"], 1)
                if what == "ga":
                    act.wait_ge(sm["ga_done"], eno(p, e) + 2)
                    act_(xe[:, :], ps[0:SLOTS, 6 * 512:8 * 512], ACT.Copy).then_inc(sm["xe_ready"], 1)
                if what == "xt":
                    act.wait_ge(sm["xt_done"], eno(p, e) + 2)
                    b, q = (u + 1) % 2, (u + 1) % 4
                    act_(oht[:, q * T:(q + 1) * T], bank(7, 0, T), ACT.Copy)
                    act_(gs[:, q:q + 1], bank(7, T, 1), ACT.Copy)
                    act_(xf[b][:, :], bank(6, GU_UNSPLIT * SLOTS, SLOTS), ACT.Copy)
                    act_(halves(xs[b])[:, :, 0, :], tiles(bank(6)), ACT.Copy).then_inc(sm["xt_hi"], 1)
                if what == "low":
                    act.wait_ge(sm["split_used"], last_gu(p, e) + NB)
                    act_(comb[SLOTS:P, :], ps[SLOTS:P, 0:4 * 512], ACT.Copy).then_inc(sm["cb_ready"], 1)
                if what == "glu":
                    act.wait_ge(sm["gc_ready"], eno(p, e) + 1)
                    act_(sgm[:, :], gc[:, :], ACT.Sigmoid, scale=ALPHA).then_inc(sm["sig_done"], 1)

            act.wait_ge(sm["b_st"], 32)
            act.wait_ge(sm["npass_ready"], 1)
            moe_steps(act, hi, task, BEGIN_ACT, FIRST_ACT, PLAN_ACT, LAST_ACT)
            act_(small[:, 63:64], small[:, 60:61], ACT.Sqrt).then_inc(sm["xrms"], 1)
            own("xrms")
            added = passes(act) * (TB * EXPERTS)
            for tb in range(TB):
                act.wait_ge(sm["sc_added"], added + tb)
                act_(ring[:, 0:D], xacc[:, tb * D:(tb + 1) * D], ACT.Square, accum_out=small[:, 20 + tb:21 + tb]).then_inc(sm["sumsq"], 1)
                own("sumsq")
                act_(small[:, 22 + tb:23 + tb], small[:, 20 + tb:21 + tb], ACT.Sqrt, scale=1.0 / D, bias=small[:, 60:61]).then_inc(sm["xrms"], 1)
                own("xrms")

        @block.vector
        def _(dve):
            link, own = Chain(dve, dve_chain), Own(dve)
            link(V.memset(small[:, 60:61], RMS_EPS))
            link(V.memset(small[:, 61:62], LN_EPS))
            V.memset(small[:, 62:63], GN_EPS).then_inc(sm["eps_ready"], 1)
            own("eps_ready")
            for b in range(2):
                for i in range(3):
                    last = V.memset(zp[b][i][:, 0:1], 0.0)
            last.then_inc(sm["pads"], 1)
            own("pads")
            dve.wait_ge(sm["xrms"], 2)
            link(V.reciprocal(small[:, 4:6], small[:, 2:4]))
            for tb in range(TB):
                V.tensor_scalar(xn[:, tb * D:(tb + 1) * D], xacc[:, tb * D:(tb + 1) * D], small[:, 4 + tb:5 + tb], None, MUL).then_inc(sm["xn_ready"], 1)
                own("xn_ready")
            dve.wait_ge(sm["vec_ps"], 1)
            V.tensor_copy(vec[:, :], bank(4, 0, VROWS)).then_inc(sm["vec_ready"], 1)
            own("vec_ready")
            dve.wait_ge(sm["vec_ready"], 1)
            for tb in range(TB):
                dve.wait_ge(sm["h_ps"], tb + 1)
                V.tensor_tensor(hT[:, :].rearrange("p (k t) -> p k t", k=KT)[:, :, tb * P:(tb + 1) * P],
                                ps[:, tb * 1024:(tb + 1) * 1024].rearrange("p (k t) -> p k t", k=KT),
                                vec[:, 0:KT].unsqueeze(2).to_broadcast([P, KT, P]), MUL).then_inc(sm["h_ready"], 1)
                own("h_ready")

            def mix(src, dst, col, count, rows=P, done=None):
                dve.wait_ge(sm["z_copied"], count)
                r = slice(0, rows)
                link(V.tensor_tensor(tmp[r, :], src[r, 0:T], src[r, 1:T + 1], SUB))
                ins = V.scalar_tensor_tensor(dst[r, :], tmp[r, :], col[r, :], src[r, 1:T + 1], MUL, ADD)
                ins.then_inc(sm[done], 1)
                own(done)

            for i in range(3):
                mix(zp[0][i], zs[0][i], vcol("mix_lora", i), i + 1, 32 if i == 2 else P, "lo_mixed")
            dve.wait_ge(sm["up_sig"], KT)

            def gram_evac(c):
                dve.wait_ge(sm["gram_done"], c + 1)
                for hh in range(2):
                    q0 = (2 * c + hh) * NCH
                    for rows, dst in ((slice(0, CH), gup), (slice(CH, P), arg)):
                        last = V.tensor_tensor(dst[rows, q0 * P:(q0 + NCH) * P].rearrange("p (q t) -> p q t", q=NCH),
                                               bank(4 + hh, 0, 512, rows).rearrange("p (q t) -> p q t", q=NCH),
                                               C("gmask", rows).unsqueeze(1).to_broadcast([CH, NCH, P]), MUL)
                last.then_inc(sm["gram_out"], 1)
                own("gram_out")

            for c in range(KT):
                b = c % 2
                zk, zr, zv = zs[b][1], zs[b][0], zs[b][2]
                cols = slice(c * T, (c + 1) * T)
                if c >= 2:
                    dve.wait_ge(sm["tr_done"], c - 1)
                mix(zp[b][1], zk, vcol("mix_k", c), 3 + 3 * c + 1, P, "zk_ready")
                mix(zp[b][0], zr, vcol("mix_r", c), 3 + 3 * c + 2, P, "zr_ready")
                link(V.tensor_tensor_scan(csum[:, :], C("carry"), sw[:, cols], 0.0, MUL, ADD))
                link(V.tensor_tensor(csump[:, :], csum[:, :], sw[:, cols], SUB))
                dve.sem_inc(sm["csum_ready"], 1)
                dve.wait_ge(sm["zk_ready"], c + 1)
                dve.wait_ge(sm["zr_ready"], c + 1)
                link(V.tensor_scalar(tmp[:, :], sa[:, cols], 1.0, vcol("k_a", c), SUB, MUL))
                link(V.scalar_tensor_tensor(kp[:, :], tmp[:, :], 1.0, zk[:, :], ADD, MUL))
                V.scalar_tensor_tensor(qb[b][:, :], zr[:, :], vcol("r_k", c), kp[:, :], MUL, MUL).then_inc(sm["q_ready"], 1)
                own("q_ready")
                mix(zp[b][2], zv, vcol("mix_v", c), 3 + 3 * c + 3, P, "zs_used")
                dve.wait_ge(sm["nrm_ready"], c + 1)
                link(V.tensor_scalar(nrm[:, :], nrm[:, :], 1e-12, None, ALU.max))
                link(V.reciprocal(nrm[:, :], nrm[:, :]))
                link(V.scalar_tensor_tensor(kr[:, :], zk[:, :], vcol("k_k", c), nrm[:, :], MUL, MUL))
                link(V.tensor_tensor(tmp[:, :], kr[:, :], sa[:, cols], MUL))
                dve.wait_ge(sm["dec_ready"], c + 1)
                ar_v = ar[b][:, :].rearrange("p (q w t) -> p q w t", q=NCH, w=2)
                bf_v = bf[b][:, :].rearrange("p (q w t) -> p q w t", q=NCH, w=2)
                q3 = lambda a: a.rearrange("p (q t) -> p q t", q=NCH)
                link(V.scalar_tensor_tensor(ar_v[:, :, 0, :], q3(kr[:, :]), -1.0, q3(decp[:, :]), MUL, MUL))
                link(V.tensor_tensor(ar_v[:, :, 1, :], q3(zr[:, :]), q3(dec[:, :]), MUL))
                link(V.tensor_tensor(bf_v[:, :, 0, :], q3(tmp[:, :]), q3(inv[:, :]), MUL))
                V.tensor_tensor(bf_v[:, :, 1, :], q3(kp[:, :]), q3(inv[:, :]), MUL).then_inc(sm["feat_ready"], 1)
                own("feat_ready")
                if c:
                    gram_evac(c - 1)
            gram_evac(KT - 1)
            meet(dve, 1)
            xl_v = xl[:, :].rearrange("p (n s) -> p n s", n=32)
            al_v = al[:, :].rearrange("p (s t) -> p s t", s=32)
            link(V.memset(xl[:, :], 0.0))
            link(V.memset(xl[:, 0:1024:33], 1.0))
            dve.wait_ge(sm["lanes_ld"], 16)
            for t in range(1, 32):
                pr = prod[:, 0:t * t].rearrange("p (n s) -> p n s", n=t)
                link(V.tensor_tensor(pr, xl_v[:, 0:t, 0:t], al_v[:, 0:t, t].unsqueeze(1).to_broadcast([P, t, t]), MUL))
                link(V.tensor_reduce(xl_v[:, 0:t, t], pr, AX.X, ADD))
            dve.sem_inc(sm["lanes_done"], 1)
            dve.wait_ge(sm["wst_copied"], 1)
            V.tensor_tensor(wst[:, :].rearrange("p (g i) -> p g i", g=GROUPS), wst[:, :].rearrange("p (g i) -> p g i", g=GROUPS),
                            C("causal").unsqueeze(1).to_broadcast([P, GROUPS, P]), MUL).then_inc(sm["wst_ready"], 1)
            own("wst_ready")
            dve.wait_ge(sm["bc_in"], 64)
            dve.wait_ge(sm["pb_out"], 4)
            for tb in range(TB):
                v_ = vsb[:, tb * D:(tb + 1) * D]
                link(V.tensor_reduce(small[:, 14 + tb:15 + tb], v_, AX.X, ADD))
                link(V.tensor_scalar(small[:, 16 + tb:17 + tb], small[:, 14 + tb:15 + tb], 1.0 / D, None, MUL))
                V.tensor_scalar(v_, v_, small[:, 16 + tb:17 + tb], None, SUB).then_inc(sm["ln_mean"], 1)
                own("ln_mean")
            dve.wait_ge(sm["ln_sqrt"], 1)
            link(V.reciprocal(small[:, 18:20], small[:, 12:14]))
            for tb in range(TB):
                v_ = vsb[:, tb * D:(tb + 1) * D]
                link(V.scalar_tensor_tensor(v_, v_, small[:, 18 + tb:19 + tb], bc[:, 0:D], MUL, MUL))
                V.tensor_tensor(v_, v_, bc[:, D:2 * D], ADD).then_inc(sm["vn_ready"], 1)
                own("vn_ready")
            def spatial(tb):
                dve.wait_ge(sm["pb_out"], 8)
                dve.wait_ge(sm["sp_done"], tb + 1)
                for g in range(GROUPS):
                    o = mb[:, tb * D + g * P:tb * D + (g + 1) * P]
                    last = V.scalar_tensor_tensor(o, ps[:, 6 * 512 + g * P:6 * 512 + (g + 1) * P], vcol("b_sp", g), o, ADD, MUL)
                last.then_inc(sm["sp_out"], 1)
                own("sp_out")

            spatial(0)
            spatial(1)
            dve.wait_ge(sm["xt_in"], 32)
            gup_q = gup[:, :].rearrange("s (q t) -> s q t", q=PAIRS)
            V.transpose(x1w[0:32, :].rearrange("s (q t) -> s q t", q=PAIRS), gup_q[0:32, :, 0:32]).then_inc(sm["x1_ready"], 1)
            own("x1_ready")

            def x21(r):
                dve.wait_ge(sm["x21_done"], r + 1)
                V.tensor_copy(gup_q[0:32, 16 * r:16 * r + 16, 32:64],
                              bank(5, 0, 512, slice(0, 32)).rearrange("s (q t) -> s q t", q=16)).then_inc(sm["x21_out"], 1)
                own("x21_out")

            def gate_bias(n, tb):
                m_ = 2 * n + tb
                dve.wait_ge(sm["pb_done"], m_ + 1)
                dst = (prod[:, (m_ % 2) * 512:(m_ % 2) * 512 + 512] if n < 6
                       else vsb[:, tb * D + 512 * (n % 2):tb * D + 512 * (n % 2) + 512])
                bias = bc[:, (3 if n < 6 else 2) * D + 512 * (n % 2):(3 if n < 6 else 2) * D + 512 * (n % 2) + 512]
                V.tensor_tensor(dst, bank(m_ % 4), bias, ADD).then_inc(sm["gate_pre"], 1)
                own("gate_pre")
                if n < 6:
                    dve.wait_ge(sm["gate_sig"], m_ - 8 + 1)
                    o = mb[:, tb * D + 512 * (n % 2):tb * D + 512 * (n % 2) + 512]
                    link(V.tensor_tensor(o, o, dst, MUL))

            for n, tb in ((4, 0), (4, 1), (5, 0), (5, 1), (6, 0)):
                gate_bias(n, tb)
            x21(0)
            gate_bias(6, 1)
            x21(1)
            gate_bias(7, 0)
            x21(2)
            gate_bias(7, 1)
            x21(3)
            meet(dve, 2)
            for g in range(2):
                V.memset(zst[0:HD, g * 512:(g + 1) * 512], 0.0).then_inc(sm["s_out"], 1)
                own("s_out")
            h3 = lambda a: a.rearrange("p (h i) -> p h i", h=HEADS)
            per_head = lambda a: a.unsqueeze(2).to_broadcast([P, HEADS, HD])

            def extras(tb):
                v_ = vtok[:, tb * D:(tb + 1) * D]
                dve.wait_ge(sm["v_put"], 2 * tb + 2)
                if tb == 0:
                    dve.wait_ge(sm["bc_in"], 112)
                link(V.tensor_tensor(h3(v_), h3(v_), per_head(bonus[:, tb * HEADS:(tb + 1) * HEADS]), MUL))
                link(V.tensor_tensor(v_, v_, bc[:, D:2 * D], ADD))
                dve.wait_ge(sm["glora_done"], tb + 1)
                g_ = vsb[:, tb * D:(tb + 1) * D]
                V.tensor_tensor(g_, g_, ps[:, 4 * 512:6 * 512], MUL).then_inc(sm["glora_out"], 1)
                own("glora_out")

            mean = small[:, 144:160]

            def gn_centre(tb):
                y = ysb[:, tb * D:(tb + 1) * D]
                dve.wait_ge(sm["y_out"], tb + 1)
                link(V.tensor_reduce(mean, h3(y), AX.X, ADD))
                link(V.tensor_scalar(mean, mean, 1.0 / HD, None, MUL))
                V.tensor_tensor(h3(y), h3(y), per_head(mean), SUB).then_inc(sm["yc_ready"], 1)
                own("yc_ready")

            def gn_var(tb):
                dve.wait_ge(sm["yc_sq"], tb + 1)
                V.tensor_reduce(small[:, 112 + 16 * tb:128 + 16 * tb], h3(yt), AX.X, ADD).then_inc(sm["yvar"], 1)
                own("yvar")

            def gn_weight(tb):
                y = ysb[:, tb * D:(tb + 1) * D]
                link(V.tensor_tensor(y, y, bc[:, 0:D], MUL))

            def gn_rest(tb):
                y, std = ysb[:, tb * D:(tb + 1) * D], small[:, 80 + 16 * tb:96 + 16 * tb]
                dve.wait_ge(sm["gn_sqrt"], tb + 1)
                link(V.reciprocal(std, std))
                link(V.tensor_tensor(h3(y), h3(y), per_head(std), MUL))
                link(V.tensor_tensor(y, y, vtok[:, tb * D:(tb + 1) * D], ADD))
                link(V.tensor_tensor(y, y, vsb[:, tb * D:(tb + 1) * D], MUL))
                V.tensor_tensor(y, y, mb[:, tb * D:(tb + 1) * D], ADD).then_inc(sm["m_ready"], 1)
                own("m_ready")

            for c in range(NCH):
                for g in range(2):
                    dve.wait_ge(sm["u_done"], 2 * c + g + 1)
                    if c:
                        dve.wait_ge(sm["y_done"], 2 * c)
                    V.tensor_copy(uv[0:CH, g * 512:(g + 1) * 512], bank(2 + g, 0, 512, slice(0, CH))).then_inc(sm["u_out"], 1)
                    own("u_out")
                if c == NCH - 1:
                    break
                for g in range(2):
                    dve.wait_ge(sm["s_done"], 2 * c + g + 1)
                    s_in = zst[0:HD, c * D + g * 512:c * D + (g + 1) * 512]
                    s_out = zst[0:HD, (c + 1) * D + g * 512:(c + 1) * D + (g + 1) * 512]
                    link(V.tensor_tensor(s_out, bank(2 + g, 0, 512, slice(0, HD)), s_in, ADD))
                    pl = plast[:, :].rearrange("j (h c) -> j h c", c=NCH)[:, 8 * g:8 * g + 8, c]
                    so = s_out.rearrange("j (h i) -> j h i", h=8)
                    V.tensor_tensor(so, so, pl.unsqueeze(2).to_broadcast([HD, 8, HD]), MUL).then_inc(sm["s_out"], 1)
                    own("s_out")
                if c < 2:
                    extras(c)
                else:
                    gn_centre(0)
                    gn_var(0)
                    gn_weight(0)
            gn_rest(0)
            gn_centre(1)
            gn_var(1)
            gn_weight(1)
            gn_rest(1)

            def x2(tb):
                for half in range(2):
                    dve.wait_ge(sm["pb_done"], 2 * NBC + 2 * tb + half + 1)
                    o = xacc[:, tb * D + 512 * half:tb * D + 512 * half + 512]
                    V.tensor_tensor(o, o, bank(2 * tb + half), ADD).then_inc(sm["o_out"], 1)
                    own("o_out")
                dve.wait_ge(sm["xrms"], 3 + tb)
                link(V.reciprocal(small[:, 24 + tb:25 + tb], small[:, 22 + tb:23 + tb]))
                V.scalar_tensor_tensor(h2[:, tb * D:(tb + 1) * D], xacc[:, tb * D:(tb + 1) * D], small[:, 24 + tb:25 + tb],
                                       bc[:, 2 * D:3 * D], MUL, MUL).then_inc(sm["h2_ready"], 1)
                own("h2_ready")

            def h2_low(tb):
                dve.wait_ge(sm["h2_hi"], tb + 1)
                c_ = slice(tb * D, (tb + 1) * D)
                link(V.tensor_tensor(h2l[:, c_], h2[:, c_], h2h[:, c_].bitcast(fp32), SUB))

            def top4(tb):
                e_ = slice(tb * EXPERTS, (tb + 1) * EXPERTS)
                m8, i8, f8 = mx[:, 8 * tb:8 * tb + 8], ix[:, 8 * tb:8 * tb + 8], ixf[:, 8 * tb:8 * tb + 8]
                dve.wait_ge(sm["lg_done"], tb + 1)
                link(V.tensor_copy(lg[:, e_], bank(6 + tb, 0, EXPERTS)))
                link(V.max(m8, lg[:, e_]))
                V.tensor_scalar(small[:, 30 + tb:31 + tb], m8[:, 0:1], -1.0, None, MUL).then_inc(sm["neg_max"], 1)
                own("neg_max")
                link(V.max_index(i8, m8, lg[:, e_]))
                link(V.tensor_copy(f8, i8))
                link(V.tensor_scalar(mask[:, e_], C("iota_exp"), f8[:, 0:1], None, ALU.is_equal))
                for k in range(1, TOPK):
                    link(V.scalar_tensor_tensor(mask[:, e_], C("iota_exp"), f8[:, k:k + 1], mask[:, e_], ALU.is_equal, ADD))
                dve.sem_inc(sm["mask_ready"], 1)

            def gates(tb):
                e_ = slice(tb * EXPERTS, (tb + 1) * EXPERTS)
                dve.wait_ge(sm["e_out"], tb + 1)
                link(V.tensor_tensor(el[:, e_], el[:, e_], mask[:, e_], MUL))
                link(V.tensor_reduce(small[:, 32 + tb:33 + tb], el[:, e_], AX.X, ADD))
                link(V.reciprocal(small[:, 34 + tb:35 + tb], small[:, 32 + tb:33 + tb]))
                V.tensor_scalar(gate[:, e_], el[:, e_], small[:, 34 + tb:35 + tb], None, MUL).then_inc(sm["gate_ready"], 1)
                own("gate_ready")

            def gate_columns(tb):
                dve.wait_ge(sm["gt_ps"], tb + 1)
                V.tensor_copy(gt[:, tb * P:(tb + 1) * P], bank(6 + tb, 256, P, slice(0, EXPERTS))).then_inc(sm["gt_ready"], 1)
                own("gt_ready")

            def down_bias(tb):
                dve.wait_ge(sm["bd_done"], tb + 1)
                o = xacc[:, tb * D:(tb + 1) * D]
                link(V.tensor_tensor(o, o, ps[:, 2 * tb * 512:(2 * tb + 2) * 512], ADD))

            x2(0)
            dve.wait_ge(sm["b_hi"], 1)
            V.tensor_tensor(bgl[:, :], bg[:, :], bgh[:, :].bitcast(fp32), SUB).then_inc(sm["b_split"], 1)
            own("b_split")
            h2_low(0)
            top4(0)
            x2(1)
            gates(0)
            gate_columns(0)
            h2_low(1)
            top4(1)
            gates(1)
            dve.wait_ge(sm["pos_done"], 1)
            link(V.scalar_tensor_tensor(posm[:, :], bank(6, 0, TB * EXPERTS), 1.0, mask[:, :], ADD, MUL))
            link(V.tensor_scalar(posm[:, :], posm[:, :], -1.0, None, ADD))
            link(V.reduce_max(small[:, 40:41], bank(6, 128, EXPERTS), AX.X))
            link(V.tensor_scalar(small[:, 41:42], small[:, 40:41], SLOTS + 0.5, 1.0, ALU.is_gt, ADD))
            for k in range(2, T // SLOTS):
                link(V.scalar_tensor_tensor(small[:, 41:42], small[:, 40:41], k * SLOTS + 0.5, small[:, 41:42], ALU.is_gt, ADD))
            V.tensor_copy(npass[:, 0:1], small[:, 41:42]).then_inc(sm["npass_ready"], 1)
            own("npass_ready")
            gate_columns(1)
            dve.sem_inc(sm["sc_added"], 1)
            for slot in range(RING):
                dve.sem_inc(ring_read[slot], 1)
            down_bias(0)
            down_bias(1)

            halves = lambda t: t[:, :].rearrange("p (k two s) -> p k two s", k=KT, two=2)
            tiles = lambda a: a.rearrange("p (k s) -> p k s", k=KT)

            def lo(p, e, s, u):
                if s in UNSPLIT:
                    return
                slot, fill = ring_at(p, e, s)
                buf = split_buf(e, s, u)
                dve.wait_ge(sm["hi_ready"], split_no(p, e, s) + 1)
                V.tensor_tensor(wl[buf][:, :], ring[:, slot * PIECE:(slot + 1) * PIECE], wh[buf][:, :].bitcast(fp32), SUB).then_inc(ring_read[slot], 1)

            def task(p, e, what, u):
                n = eno(p, e)
                if what == "oh":
                    if not (isinstance(e, int) and e < 0):
                        dve.wait_ge(sm["xt_done"], n + 1)
                    else:
                        dve.wait_ge(sm["pos_moved"], p + 1)
                    for tb in range(TB):
                        last = V.tensor_scalar(oh[:, tb * S2:(tb + 1) * S2], C("iota_slot"),
                                               col(posm, tb, e + 1), None, ALU.is_equal)
                    last.then_inc(sm["oh_ready"], 1)
                if what == "y":
                    dve.wait_ge(sm["y_hi"], n - 1)
                    V.scalar_tensor_tensor(yl[:, :], ps[:, 4 * 512:6 * 512], gs[:, (u - 2) % 4:(u - 2) % 4 + 1],
                                           yh[:, :].bitcast(fp32), MUL, SUB).then_inc(sm["y_lo"], 1)
                if what in ("sc0", "sc1"):
                    tb = int(what[2])
                    dve.wait_ge(sm["sc_done"], 2 * n - 4 + tb + 1)
                    dve.wait_ge(sm["sc_added"], 2 * n - 4 + tb + 1)
                    o = xacc[:, tb * D:(tb + 1) * D]
                    b = scatter_bank(e, tb)
                    V.tensor_tensor(o, o, ps[:, b * 512:(b + 2) * 512], ADD).then_inc(sm["sc_added"], 1)
                if what == "at":
                    dve.wait_ge(sm["at_hi"], n)
                    V.tensor_tensor(halves(as_)[:, :, 1, :], tiles(bank(6)), halves(as_)[:, :, 0, :].bitcast(fp32), SUB).then_inc(sm["at_lo"], 1)
                if what == "xt":
                    dve.wait_ge(sm["xt_hi"], n + 2)
                    b = (u + 1) % 2
                    V.tensor_tensor(halves(xs[b])[:, :, 1, :], tiles(bank(6)), halves(xs[b])[:, :, 0, :].bitcast(fp32), SUB).then_inc(sm["xt_lo"], 1)
                if what == "glu":
                    dve.wait_ge(sm["comb_used"], n + 2)
                    pairs = ps[0:SLOTS, 0:4 * 512].rearrange("p (f two) -> p two f", two=2)
                    V.tensor_scalar(gc[:, :], pairs[:, 0, :], LIMIT, None, ALU.min).then_inc(sm["gc_ready"], 1)
                    V.tensor_scalar(uc[:, :], pairs[:, 1, :], LIMIT, -LIMIT, ALU.min, ALU.max).then_inc(sm["gu_read"], 1)
                if what == "act":
                    dve.wait_ge(sm["gu_read"], n + 1)
                    V.scalar_tensor_tensor(uc[:, :], uc[:, :], 1.0, gc[:, :], ADD, MUL).then_inc(sm["ug_ready"], 1)
                    dve.wait_ge(sm["ug_ready"], n)
                    dve.wait_ge(sm["sig_done"], n)
                    V.tensor_tensor(acts[:, :], uc[:, :], sgm[:, :], MUL).then_inc(sm["act_ready"], 1)
                if what == "next":
                    V.tensor_scalar(posm[:, :], posm[:, :], float(-SLOTS), None, ADD).then_inc(sm["pos_moved"], 1)

            dve.sem_inc(sm["pos_moved"], 1)
            dve.sem_inc(sm["gu_read"], 1)
            moe_steps(dve, lo, task, BEGIN_DVE, FIRST_DVE, PLAN_DVE, LAST_DVE)
            dve.wait_ge(sm["nf_in"], 16)
            for tb in range(TB):
                dve.wait_ge(sm["xrms"], 6 + tb)
                link(V.reciprocal(small[:, 24 + tb:25 + tb], small[:, 22 + tb:23 + tb]))
                o = xacc[:, tb * D:(tb + 1) * D]
                V.scalar_tensor_tensor(o, o, small[:, 24 + tb:25 + tb], nf[:, :], MUL, MUL).then_inc(sm["fin_ready"], 1)

        @block.tensor
        def _(pe):
            mm, tr = E.matmul, E.transpose
            ident = C("ident")
            hv = hT[:, :].rearrange("p (k t) -> p k t", k=KT)
            pe.wait_ge(misc[0], 16)
            for tb in range(TB):
                pe.wait_ge(sm["xn_ready"], tb + 1)
                for k in range(KT):
                    last = tr(ps[:, tb * 1024 + k * P:tb * 1024 + (k + 1) * P], xn[:, tb * D + k * P:tb * D + (k + 1) * P], ident)
                last.then_inc(sm["h_ps"], 1)
            pe.wait_ge(misc[1], 16 * 6)
            pe.wait_ge(sm["rows_in"], 16 * 6)
            tr(bank(4, 0, VROWS), vrow[0:VROWS, :], ident[0:VROWS, 0:VROWS]).then_inc(sm["vec_ps"], 1)
            wa_v = wa[:, :].rearrange("p (s k n) -> p s k n", s=8, k=KT)
            pe.wait_ge(sm["h_ready"], 2)

            def project(n):
                w = a_cols[n][1]
                pe.wait_ge(wa_full[n % 8], 16 * (n // 8 + 1))
                if n >= 2:
                    pe.wait_ge(sm["z_copied"], n - 1)
                for k in range(KT):
                    last = mm(bank(n % 2, 0, T, slice(0, w)), wa_v[:, n % 8, k, 0:w], hv[:, k, :], start=k == 0, stop=k == KT - 1)
                last.then_inc(sm["proj_done"], 1)

            for n in range(5):
                project(n)
            pe.wait_ge(sm["lo_act"], 1)
            pe.wait_ge(sm["upw_in"], 32)
            for c in range(KT):
                if c >= 2:
                    pe.wait_ge(sm["up_sig"], c - 1)
                for b_, rows in ((2, slice(0, LORA)), (3, slice(LORA, P))):
                    last = mm(bank(b_ + 2 * (c % 2), 0, T), upw[rows, c * P:(c + 1) * P], zs[0][0][rows, :], start=True, stop=True)
                last.then_inc(sm["up_done"], 1)

            def products(c):
                b = c % 2
                pe.wait_ge(sm["feat_ready"], c + 1)
                if c:
                    pe.wait_ge(sm["gram_out"], c)
                for q in range(NCH):
                    for hh in range(2):
                        rows = slice(HD * hh, HD * hh + HD)
                        last = mm(bank(4 + hh, q * P, P), bf[b][rows, q * P:(q + 1) * P], ar[b][rows, q * P:(q + 1) * P], start=True, stop=True)
                last.then_inc(sm["gram_done"], 1)
                if c:
                    pe.wait_ge(sm["tr_out"], c)
                for q in range(NCH):
                    tr(bank(6, q * P, P), bf[b][:, q * P:(q + 1) * P], ident)
                pe.wait_ge(sm["zs_used"], c + 1)
                for tb in range(TB):
                    tr(bank(7, tb * P, P), zs[b][2][:, tb * P:(tb + 1) * P], ident)
                for tb in range(TB):
                    last = mm(bank(3, tb * HEADS + 2 * c, 2), qb[b][:, tb * P:(tb + 1) * P], C("of_head"), start=True, stop=True)
                last.then_inc(sm["tr_done"], 1)

            for c in range(KT):
                for n in range(max(3 + 3 * c, 5), 6 + 3 * c):
                    project(n)
                if c == 0:
                    pe.wait_ge(sm["up_sig"], KT)
                    pe.wait_ge(sm["lo_act"], 2)
                pe.wait_ge(sm["sq_ready"], c + 1)
                mm(bank(2, 0, T), C("headones"), sqb[:, :], start=True, stop=True).then_inc(sm["norm_done"], 1)
                if c:
                    products(c - 1)
            wb_v = wb[:, :].rearrange("p (s k n) -> p s k n", s=2, k=KT)

            def chunk(n, tb):
                m_ = 2 * n + tb
                pe.wait_ge(wb_full[n % 2], 16 * (n // 2 + 1))
                if m_ >= 12:
                    pe.wait_ge(sm["gate_pre"], m_ - 12 + 1)
                elif m_ >= 4:
                    pe.wait_ge(sm["pb_out"], m_ - 4 + 1)
                for k in range(KT):
                    last = mm(bank(m_ % 4), hv[:, k, tb * P:(tb + 1) * P], wb_v[:, (n + 1) % 2, k, :], start=k == 0, stop=k == KT - 1)
                last.then_inc(sm["pb_done"], 1)

            pe.wait_ge(sm["z_copied"], NA)
            chunk(0, 0)
            chunk(0, 1)
            products(KT - 1)
            meet(pe, 1)
            chunk(1, 0)
            chunk(1, 1)
            pe.wait_ge(sm["ws_in"], 16)
            for g in range(GROUPS):
                last = tr(ps[:, 4 * 512 + g * P:4 * 512 + (g + 1) * P], wsr[:, g * P:(g + 1) * P], ident)
            last.then_inc(sm["wst_ps"], 1)
            for n in (2, 3):
                for tb in range(TB):
                    chunk(n, tb)
            gup_q = gup[:, :].rearrange("s (q t) -> s q t", q=PAIRS)

            def with_x11(r):
                if r:
                    pe.wait_ge(sm["w1_out"], r)
                else:
                    pe.wait_ge(sm["x1_ready"], 1)
                    pe.wait_ge(sm["wst_copied"], 1)
                for q in range(16):
                    pr = 16 * r + q
                    last = mm(bank(4, 32 * q, 32, slice(32, 64)), gup_q[0:32, pr, 32:64], x1w[0:32, pr * 32:(pr + 1) * 32], start=True, stop=True)
                last.then_inc(sm["w1_done"], 1)

            def with_x22(r):
                pe.wait_ge(sm["w1_out"], r + 1)
                if r:
                    pe.wait_ge(sm["x21_out"], r)
                for q in range(16):
                    pr = 16 * r + q
                    last = mm(bank(5, 32 * q, 32, slice(0, 32)), x1w[32:64, pr * 32:(pr + 1) * 32], gup_q[32:64, pr, 32:64], start=True, stop=True)
                last.then_inc(sm["x21_done"], 1)

            def spatial(tb):
                if tb:
                    pe.wait_ge(sm["sp_out"], tb)
                else:
                    pe.wait_ge(sm["wst_ready"], 1)
                pe.wait_ge(sm["vn_ready"], tb + 1)
                for g in range(GROUPS):
                    last = mm(ps[:, 6 * 512 + g * P:6 * 512 + (g + 1) * P], wst[:, g * P:(g + 1) * P],
                              vsb[:, tb * D + g * P:tb * D + (g + 1) * P], start=True, stop=True)
                last.then_inc(sm["sp_done"], 1)

            chunk(4, 0)
            chunk(4, 1)
            spatial(0)
            chunk(5, 0)
            spatial(1)
            chunk(5, 1)
            with_x11(0)
            chunk(6, 0)
            with_x22(0)
            with_x11(1)
            chunk(6, 1)
            with_x22(1)
            with_x11(2)
            chunk(7, 0)
            with_x22(2)
            with_x11(3)
            chunk(7, 1)
            with_x22(3)
            meet(pe, 2)
            def glora(tb):
                if tb:
                    pe.wait_ge(sm["glora_out"], tb)
                pe.wait_ge(sm["gu_in"], 32)
                for half in range(2):
                    o = bank(4 + half)
                    mm(o, sg[:, tb * P:(tb + 1) * P], gu1[:, 512 * half:512 * half + 512], start=True, stop=False)
                    last = mm(o, sg[0:32, T + tb * P:T + (tb + 1) * P], gu2[:, 512 * half:512 * half + 512], start=False, stop=True)
                last.then_inc(sm["glora_done"], 1)

            for c in range(NCH):
                y0 = CH * (c % 2)
                pe.wait_ge(sm["v_put"], c + 1)
                for g in range(2):
                    pe.wait_ge(sm["s_out"], 2 * c + g + 1)
                    if c:
                        pe.wait_ge(sm["r_out"], 2 * (c - 1) + g + 1)
                    for i in range(8):
                        h = 8 * g + i
                        q = h * NCH + c
                        last = mm(bank(g, i * HD, HD, slice(0, CH)), arg[:, q * P:q * P + CH], zst[:, c * D + h * HD:c * D + (h + 1) * HD], start=True, stop=True)
                    last.then_inc(sm["r_done"], 1)
                for g in range(2):
                    pe.wait_ge(sm["r_out"], 2 * c + g + 1)
                    for i in range(8):
                        h = 8 * g + i
                        q = h * NCH + c
                        last = mm(bank(2 + g, i * HD, HD, slice(0, CH)), gup[:, q * P:q * P + CH], rhs[:, h * HD:(h + 1) * HD], start=True, stop=True)
                    last.then_inc(sm["u_done"], 1)
                pe.wait_ge(sm["uv_v"], c + 1)
                for g in range(2):
                    pe.wait_ge(sm["u_out"], 2 * c + g + 1)
                    if c == NCH - 1:
                        continue
                    for i in range(8):
                        h = 8 * g + i
                        q = h * NCH + c
                        last = mm(bank(2 + g, i * HD, HD, slice(0, HD)), bk[:, q * HD:(q + 1) * HD], uv[:, h * HD:(h + 1) * HD], start=True, stop=True)
                    last.then_inc(sm["s_done"], 1)
                if c == 2:
                    pe.wait_ge(sm["y_out"], 1)
                for g in range(2):
                    for i in range(8):
                        h = 8 * g + i
                        q = h * NCH + c
                        o = bank(6 + g, i * HD, HD, slice(y0, y0 + CH))
                        mm(o, arg[:, q * P + CH:(q + 1) * P], zst[:, c * D + h * HD:c * D + (h + 1) * HD], start=True, stop=False)
                        last = mm(o, gup[:, q * P + CH:(q + 1) * P], uv[0:CH, h * HD:(h + 1) * HD], start=False, stop=True)
                    last.then_inc(sm["y_done"], 1)
                if c < 2:
                    glora(c)
            mv = mT[:, :].rearrange("p (k t) -> p k t", k=KT)

            def turn_block(src, tb, ready, n, done):
                pe.wait_ge(sm[ready], tb + 1)
                if n:
                    pe.wait_ge(sm["mT_ready"], n)
                for k in range(KT):
                    last = tr(ps[:, 4 * 512 + k * P:4 * 512 + (k + 1) * P], src[:, tb * D + k * P:tb * D + (k + 1) * P], ident)
                last.then_inc(sm[done], 1)

            def project_out(tb, half):
                n = NBC + half
                pe.wait_ge(wb_full[n % 2], 16 * (n // 2 + 1))
                pe.wait_ge(sm["mT_ready"], tb + 1)
                for k in range(KT):
                    last = mm(bank(2 * tb + half), mv[:, k, tb * P:(tb + 1) * P], wb_v[:, (n + 1) % 2, k, :], start=k == 0, stop=k == KT - 1)
                last.then_inc(sm["pb_done"], 1)

            def logits(tb):
                pe.wait_ge(sm["mT_ready"], 2 + tb + 1)
                pe.wait_ge(sm["late_in"], 64)
                o = bank(6 + tb, 0, EXPERTS)
                mm(o, C("ones")[0:1, :], br[:, :], start=True, stop=False)
                for k in range(KT):
                    last = mm(o, mv[:, k, tb * P:(tb + 1) * P], wr[:, k * EXPERTS:(k + 1) * EXPERTS], start=False, stop=k == KT - 1)
                last.then_inc(sm["lg_done"], 1)

            turn_block(ysb, 0, "m_ready", 0, "m_ps")
            for half in range(2):
                project_out(0, half)
            turn_block(ysb, 1, "m_ready", 1, "m_ps")
            project_out(1, 0)
            turn_block(h2, 0, "h2_ready", 2, "h2_ps")
            logits(0)
            project_out(1, 1)

            def gate_rows(tb):
                pe.wait_ge(sm["gate_ready"], tb + 1)
                tr(bank(6 + tb, 256, P, slice(0, EXPERTS)), gate[:, tb * EXPERTS:(tb + 1) * EXPERTS], ident).then_inc(sm["gt_ps"], 1)

            def down_bias(tb):
                pe.wait_ge(sm["gt_ready"], tb + 1)
                pe.wait_ge(sm["o_out"], 2 * tb + 2)
                for half in range(2):
                    last = mm(bank(2 * tb + half), gt[:, tb * P:(tb + 1) * P], bd[:, 512 * half:512 * half + 512], start=True, stop=True)
                last.then_inc(sm["bd_done"], 1)

            turn_block(h2, 1, "h2_ready", 3, "h2_ps")
            gate_rows(0)
            logits(1)
            down_bias(0)
            pe.wait_ge(sm["mask_ready"], 2)
            m0, m1_ = mask[:, 0:EXPERTS], mask[:, EXPERTS:2 * EXPERTS]
            mm(bank(6, 0, EXPERTS), C("before"), m0, start=True, stop=True)
            mm(bank(6, EXPERTS, EXPERTS), C("before"), m1_, start=True, stop=False)
            mm(bank(6, EXPERTS, EXPERTS), C("ones"), m0, start=False, stop=True)
            mm(bank(6, 128, EXPERTS), C("ones"), m0, start=True, stop=False)
            mm(bank(6, 128, EXPERTS), C("ones"), m1_, start=False, stop=True).then_inc(sm["pos_done"], 1)
            gate_rows(1)
            down_bias(1)
            pe.sem_inc(sm["split_used"], NB)
            pe.sem_inc(sm["comb_used"], 1)
            pe.wait_ge(sm["npass_ready"], 1)

            def both(o, lhs, rh, rl, start, stop):
                mm(o, lhs, rh, start=start, stop=False)
                return mm(o, lhs, rl, start=False, stop=stop)

            pe.wait_ge(sm["mrg_ready"], 1)
            pe.wait_ge(sm["zeroed"], 3)

            def turn(src):
                mm(bank(6, 0, SLOTS), src[:, 0:P], ident[0:SLOTS, 0:SLOTS], start=True, stop=True)
                for k in range(1, KT):
                    last = tr(bank(6, k * SLOTS, SLOTS), src[:, k * P:(k + 1) * P], ident[0:SLOTS, 0:SLOTS])
                return last

            def step(p, e, s, u):
                slot, fill = ring_at(p, e, s)
                buf = split_buf(e, s, u)
                if s == 0:
                    ne = eno(p, e)
                    pe.wait_ge(sm["gu_read"], ne + 1)
                    pe.wait_ge(sm["xt_lo"], ne + 1)
                if s == KT:
                    pe.wait_ge(sm["at_lo"], eno(p, e))
                    if not (isinstance(e, int) and e == 1):
                        pe.wait_ge(sm["y_lo"], eno(p, e) - 1)
                w_ = ring[:, slot * PIECE:(slot + 1) * PIECE]
                if s in UNSPLIT:
                    pe.wait_ge(ring_full[slot], fill * 16)
                    if s < KT:
                        for q in range(4):
                            w = slice(512 * q, 512 * q + 512)
                            last = mm(ps[0:SLOTS, w], xf[u % 2][:, :], w_[:, w], start=False, stop=False)
                    else:
                        for two in range(2):
                            for half in range(2):
                                w = slice(D * two + 512 * half, D * two + 512 * half + 512)
                                last = mm(bank(4 + half, 0, 512, slice(0, SLOTS)), af[:, two * SLOTS:(two + 1) * SLOTS], w_[:, w], start=False, stop=False)
                    last.then_inc(ring_read[slot], 1)
                    return
                pe.wait_ge(ring_read[slot], fill + 1)
                if s < KT:
                    for q in range(4):
                        w = slice(512 * q, 512 * q + 512)
                        last = both(ps[:, w], xs[u % 2][:, s * S2:(s + 1) * S2], wh[buf][:, w], wl[buf][:, w], s == 0, False)
                        if s == KT - 1:
                            last = mm(ps[SLOTS:P, w], zero[:, 0:SLOTS], zero[:, :], start=False, stop=True)
                else:
                    for two in range(2):
                        f = 2 * (s - KT) + two
                        for half in range(2):
                            w = slice(D * two + 512 * half, D * two + 512 * half + 512)
                            last = both(bank(4 + half), as_[:, f * S2:(f + 1) * S2], wh[buf][:, w], wl[buf][:, w], f == 0, f == KT - 1)
                last.then_inc(sm["split_used"], 1)

            def task(p, e, what, u):
                n = eno(p, e)
                if what in ("sc0", "sc1"):
                    tb = int(what[2])
                    if tb == 0:
                        pe.wait_ge(sm["y_lo"], n - 1)
                        if isinstance(e, int) and e == EXPERTS:
                            pe.wait_ge(sm["at_lo"], n)
                    elif scatter_bank(e, tb) == 6:
                        pe.wait_ge(sm["sc_added"], 2 * n - 4 + 1 + 1)
                    q = (u - 2) % 4
                    lt = oht[:, q * T + tb * P:q * T + (tb + 1) * P]
                    for half in range(2):
                        o = bank(scatter_bank(e, tb) + half)
                        mm(o, lt, yh[:, 512 * half:512 * half + 512], start=True, stop=False)
                        last = mm(o, lt, yl[:, 512 * half:512 * half + 512], start=False, stop=True)
                    last.then_inc(sm["sc_done"], 1)
                if what == "low":
                    pe.wait_ge(sm["cb_ready"], n + 1)
                    pe.wait_ge(bias_in, 16 * n + 16)
                    for q in range(4):
                        w = slice(512 * q, 512 * q + 512)
                        last = mm(ps[0:SLOTS, w], mrg[:, :], comb[:, w], start=False, stop=True)
                    last.then_inc(sm["comb_used"], 1)
                if what == "at":
                    pe.wait_ge(sm["act_ready"], n)
                    if not (isinstance(e, int) and e == 1):
                        ahead = 2 if isinstance(e, int) and e == EXPERTS else 0
                        pe.wait_ge(sm["sc_added"], 2 * n - 4 + 2 + 1 - ahead)
                    last = turn(acts)
                    last.then_inc(sm["at_done"], 1)
                if what == "ga":
                    if isinstance(e, int) and e < 0:
                        pe.wait_ge(sm["sc_added"], 2 * n + 2 + 1)
                    elif not (isinstance(e, int) and e == 0):
                        pe.wait_ge(sm["at_lo"], n)
                    pe.wait_ge(sm["oh_ready"], n + 2)
                    for half in range(2):
                        for tb in range(TB):
                            for hl, src in enumerate((h2h, h2l)):
                                last = mm(bank(6 + half, 0, 512, slice(0, SLOTS)), oh[:, tb * S2:tb * S2 + SLOTS],
                                          src[:, tb * D + 512 * half:tb * D + 512 * half + 512],
                                          start=tb == 0 and hl == 0, stop=tb == TB - 1 and hl == 1)
                    last.then_inc(sm["ga_done"], 1)
                if what == "xt":
                    pe.wait_ge(sm["xe_ready"], n + 2)
                    turn(xe)
                    for tb in range(TB):
                        tr(bank(7, tb * P, P), oh[:, tb * S2:(tb + 1) * S2].bitcast(fp32), ident)
                    for tb in range(TB):
                        last = mm(bank(7, T, 1), oh[:, tb * S2:(tb + 1) * S2].bitcast(fp32),
                                  col(gate, tb, e + 1), start=tb == 0, stop=tb == 1)
                    last.then_inc(sm["xt_done"], 1)

            moe_steps(pe, step, task, BEGIN_PE, FIRST_PE, PLAN_PE, LAST_PE)


def kernel(**inputs):
    import numpy as _np
    import concourse.bacc as _bacc
    from concourse.bass_utils import run_bass_kernel_spmd as _run

    nc = _bacc.Bacc("TRN2", target_bir_lowering=False, num_devices=1)
    arrays, args = {"cst": constants()}, {}
    for name, a in inputs.items():
        arrays[name] = _np.ascontiguousarray(a)
    for name, a in arrays.items():
        args[name] = nc.dram_tensor(name, a.shape, mybir.dt.from_np(a.dtype), kind="ExternalInput").ap()
    out = nc.dram_tensor("out", (1, T, D), mybir.dt.float32, kind="ExternalOutput").ap()
    build(nc, out=out, **args)
    r = _run(nc, [arrays], core_ids=[0])
    return r.results[0]["out"]
```
